# Optimizing a Trainium2 kernel written in Bass

```python
import math
import jax
import jax.numpy as jnp
from jax import lax
import numpy as np

D_MODEL = 1024
BATCH = 1
SEQ = 512
DEPTH = 2

CHUNK = 64
N_A_LAYERS = DEPTH // 2
N_B_LAYERS = DEPTH - N_A_LAYERS
EPS = 1e-6

RET_HEADS = 4
RET_DK = D_MODEL // RET_HEADS
RET_DV = 2 * RET_DK
RET_QK = RET_HEADS * RET_DK
RET_V = RET_HEADS * RET_DV
RET_IN = 2 * RET_QK + 2 * RET_V
ROPE_BASE = 10000.0

DIFF_HEAD_DIM = 64
DIFF_HEADS = D_MODEL // (2 * DIFF_HEAD_DIM)
DIFF_QK = DIFF_HEADS * 2 * DIFF_HEAD_DIM
DIFF_V = DIFF_HEADS * 2 * DIFF_HEAD_DIM
Q_BLOCK = 128

N_GROUPS = 4
EXPERTS_PER_GROUP = 4
N_EXPERTS = N_GROUPS * EXPERTS_PER_GROUP
TOP_K_IN_GROUP = 2
EXPERT_HIDDEN = D_MODEL
ROUTE_BLOCK = 128

kernel_name = 'yoco_retention_diffattn_hmoe_adaln'

def _rmsnorm(x, g):
    xf = x.astype(jnp.float32)
    y = xf * lax.rsqrt(jnp.mean(xf * xf, axis=-1, keepdims=True) + EPS)
    return (y * g.astype(jnp.float32)).astype(x.dtype)

def _modulate(h, shift, scale):
    return h * (1 + scale[:, None, :]) + shift[:, None, :]

def _rotary(x, pos):
    half = x.shape[-1] // 2
    inv_freq = 1.0 / (ROPE_BASE ** (jnp.arange(half, dtype=jnp.float32) / half))
    ang = pos[:, None] * inv_freq[None, :]
    cos = jnp.cos(ang)[None, :, None, :].astype(x.dtype)
    sin = jnp.sin(ang)[None, :, None, :].astype(x.dtype)
    x1, x2 = x[..., :half], x[..., half:]
    return jnp.concatenate([x1 * cos - x2 * sin, x2 * cos + x1 * sin], axis=-1)

def _retention(h, w_in, gn, w_out):
    bsz, seq, _ = h.shape
    n_chunks = seq // CHUNK
    f32 = jnp.float32
    proj = h @ w_in
    q, k, v, g = jnp.split(proj, [RET_QK, 2 * RET_QK, 2 * RET_QK + RET_V], axis=-1)
    pos = jnp.arange(seq, dtype=f32)
    q = _rotary(q.reshape(bsz, seq, RET_HEADS, RET_DK), pos).astype(f32)
    k = _rotary(k.reshape(bsz, seq, RET_HEADS, RET_DK), pos).astype(f32) * (RET_DK ** -0.5)
    v = v.reshape(bsz, seq, RET_HEADS, RET_DV).astype(f32)
    log_gamma = jnp.log1p(-jnp.exp2(-5.0 - jnp.arange(RET_HEADS, dtype=f32)))
    n = jnp.arange(CHUNK, dtype=f32)
    rel = n[:, None] - n[None, :]
    intra = jnp.where(rel >= 0, jnp.exp(jnp.maximum(rel, 0.0)[None] * log_gamma[:, None, None]), 0.0)
    q_decay = jnp.exp((n + 1.0)[None, :] * log_gamma[:, None])
    k_decay = jnp.exp((CHUNK - 1.0 - n)[None, :] * log_gamma[:, None])
    chunk_decay = jnp.exp(CHUNK * log_gamma)

    def to_chunks(t):
        return t.reshape(bsz, n_chunks, CHUNK, RET_HEADS, t.shape[-1]).transpose(1, 0, 3, 2, 4)

    def step(state, inp):
        qi, ki, vi = inp
        scores = jnp.einsum('bhnd,bhmd->bhnm', qi, ki) * intra
        out = (jnp.einsum('bhnm,bhmv->bhnv', scores, vi)
               + jnp.einsum('bhnd,bhdv->bhnv', qi * q_decay[:, :, None], state))
        state = state * chunk_decay[:, None, None] + jnp.einsum(
            'bhmd,bhmv->bhdv', ki * k_decay[:, :, None], vi)
        return state, out

    state0 = jnp.zeros((bsz, RET_HEADS, RET_DK, RET_DV), f32)
    _, o = lax.scan(step, state0, (to_chunks(q), to_chunks(k), to_chunks(v)))
    o = o.transpose(1, 0, 3, 2, 4).reshape(bsz, seq, RET_HEADS, RET_DV)
    o = o * lax.rsqrt(jnp.mean(o * o, axis=-1, keepdims=True) + EPS)
    o = o.reshape(bsz, seq, RET_V) * gn.astype(f32)
    y = jax.nn.silu(g) * o.astype(h.dtype)
    return y @ w_out

def _shared_kv(x, c_act, ada_w, ada_b, norm_g, w_kv, k_norm):
    bsz, seq, _ = x.shape
    shift, scale = jnp.split(c_act @ ada_w + ada_b, 2, axis=-1)
    h = _modulate(_rmsnorm(x, norm_g), shift, scale)
    kv = h @ w_kv
    k = _rmsnorm(kv[..., :DIFF_QK].reshape(bsz, seq, DIFF_HEADS, 2, DIFF_HEAD_DIM), k_norm)
    v = kv[..., DIFF_QK:].reshape(bsz, seq, DIFF_HEADS, 2 * DIFF_HEAD_DIM)
    return k, v

def _diff_attention(h, k, v, w_q, q_norm, lam, subln, w_out, lambda_init):
    bsz, seq, _ = h.shape
    f32 = jnp.float32
    q = _rmsnorm((h @ w_q).reshape(bsz, seq, DIFF_HEADS, 2, DIFF_HEAD_DIM), q_norm) * (DIFF_HEAD_DIM ** -0.5)
    lam_f = lam.astype(f32)
    lam_full = (jnp.exp(jnp.sum(lam_f[0] * lam_f[1])) - jnp.exp(jnp.sum(lam_f[2] * lam_f[3]))
                + lambda_init)
    n_qb = seq // Q_BLOCK
    qb = q.reshape(bsz, n_qb, Q_BLOCK, DIFF_HEADS, 2, DIFF_HEAD_DIM).transpose(1, 0, 2, 3, 4, 5)
    kpos = jnp.arange(seq)

    def block(args):
        qi, bi = args
        qpos = bi * Q_BLOCK + jnp.arange(Q_BLOCK)
        visible_end = (qpos // CHUNK + 1) * CHUNK
        mask = kpos[None, :] < visible_end[:, None]
        s = jnp.einsum('bqhtd,bkhtd->bhtqk', qi, k).astype(f32)
        p = jax.nn.softmax(jnp.where(mask, s, -jnp.inf), axis=-1)
        a = p[:, :, 0] - lam_full * p[:, :, 1]
        return jnp.einsum('bhqk,bkhv->bqhv', a.astype(v.dtype), v)

    o = lax.map(block, (qb, jnp.arange(n_qb)))
    o = o.transpose(1, 0, 2, 3, 4).reshape(bsz, seq, DIFF_HEADS, 2 * DIFF_HEAD_DIM)
    o = _rmsnorm(o, subln) * (1.0 - lambda_init)
    return o.reshape(bsz, seq, DIFF_V) @ w_out

def _hier_moe(h, w_group, b_group, w_expert, b_expert, w1, w3, w2):
    bsz, seq, dm = h.shape
    n_tok = bsz * seq
    f32 = jnp.float32
    t = h.reshape(n_tok, dm)
    g_logits = (t @ w_group + b_group).astype(f32)
    g_idx = jnp.argmax(g_logits, axis=-1)
    g_gate = jnp.take_along_axis(jax.nn.softmax(g_logits, axis=-1), g_idx[:, None], axis=-1)
    e_logits = (t @ w_expert + b_expert).astype(f32).reshape(n_tok, N_GROUPS, EXPERTS_PER_GROUP)
    e_sel = jnp.take_along_axis(e_logits, g_idx[:, None, None], axis=1)[:, 0]
    top_w, top_i = lax.top_k(jax.nn.softmax(e_sel, axis=-1), TOP_K_IN_GROUP)
    top_w = top_w / jnp.sum(top_w, axis=-1, keepdims=True) * g_gate
    expert_id = g_idx[:, None] * EXPERTS_PER_GROUP + top_i
    m = n_tok * TOP_K_IN_GROUP
    flat_e = expert_id.reshape(m)
    flat_w = top_w.reshape(m)
    flat_tok = jnp.repeat(jnp.arange(n_tok), TOP_K_IN_GROUP)
    order = jnp.argsort(flat_e)
    sorted_e = flat_e[order]
    counts = jnp.bincount(flat_e, length=N_EXPERTS)
    starts = jnp.cumsum(counts) - counts
    padded = (counts + ROUTE_BLOCK - 1) // ROUTE_BLOCK * ROUTE_BLOCK
    padded_ends = jnp.cumsum(padded)
    padded_starts = padded_ends - padded
    dest = padded_starts[sorted_e] + (jnp.arange(m) - starts[sorted_e])
    n_blocks = -(-m // ROUTE_BLOCK) + N_EXPERTS
    rows = n_blocks * ROUTE_BLOCK
    buf_tok = jnp.zeros((rows,), jnp.int32).at[dest].set(flat_tok[order])
    buf_w = jnp.zeros((rows,), f32).at[dest].set(flat_w[order])
    block_e = jnp.minimum(jnp.searchsorted(padded_ends, jnp.arange(n_blocks) * ROUTE_BLOCK, side='right'),
                          N_EXPERTS - 1)
    xb = t[buf_tok].reshape(n_blocks, ROUTE_BLOCK, dm)

    def expert_block(args):
        xi, e = args
        hid = jax.nn.silu(xi @ w1[e]) * (xi @ w3[e])
        return hid @ w2[e]

    yb = lax.map(expert_block, (xb, block_e)).reshape(rows, dm)
    out = jnp.zeros((n_tok, dm), yb.dtype).at[buf_tok].add(yb * buf_w[:, None].astype(yb.dtype))
    return out.reshape(bsz, seq, dm).astype(h.dtype)

def setup_inputs(seed: int = 0) -> dict:
    key = jax.random.key(seed)
    ks = jax.random.split(key, 32)
    f32 = jnp.float32
    D = D_MODEL

    def nrm(k, shape, fan_in):
        return jax.random.normal(k, shape, f32) * (fan_in ** -0.5)

    def gain(k, shape):
        return 1.0 + 0.02 * jax.random.normal(k, shape, f32)

    def small(k, shape):
        return 0.01 * jax.random.normal(k, shape, f32)

    return {
        'x': jax.random.normal(ks[0], (BATCH, SEQ, D), f32),
        'c': jax.random.normal(ks[1], (BATCH, D), f32),
        'ada_w': nrm(ks[2], (DEPTH, D, 6 * D), D),
        'ada_b': small(ks[3], (DEPTH, 6 * D)),
        'norm_mix': gain(ks[4], (DEPTH, D)),
        'norm_ffn': gain(ks[5], (DEPTH, D)),
        'ret_w_in': nrm(ks[6], (N_A_LAYERS, D, RET_IN), D),
        'ret_gn': gain(ks[7], (N_A_LAYERS, RET_V)),
        'ret_w_out': nrm(ks[8], (N_A_LAYERS, RET_V, D), RET_V),
        'kv_ada_w': nrm(ks[9], (D, 2 * D), D),
        'kv_ada_b': small(ks[10], (2 * D,)),
        'kv_norm': gain(ks[11], (D,)),
        'kv_w': nrm(ks[12], (D, DIFF_QK + DIFF_V), D),
        'k_norm': gain(ks[13], (DIFF_HEAD_DIM,)),
        'diff_w_q': nrm(ks[14], (N_B_LAYERS, D, DIFF_QK), D),
        'q_norm': gain(ks[15], (N_B_LAYERS, DIFF_HEAD_DIM)),
        'diff_lam': 0.1 * jax.random.normal(ks[16], (N_B_LAYERS, 4, DIFF_HEAD_DIM), f32),
        'diff_subln': gain(ks[17], (N_B_LAYERS, 2 * DIFF_HEAD_DIM)),
        'diff_w_out': nrm(ks[18], (N_B_LAYERS, DIFF_V, D), DIFF_V),
        'moe_w_group': nrm(ks[19], (DEPTH, D, N_GROUPS), D),
        'moe_b_group': small(ks[20], (DEPTH, N_GROUPS)),
        'moe_w_expert': nrm(ks[21], (DEPTH, D, N_EXPERTS), D),
        'moe_b_expert': small(ks[22], (DEPTH, N_EXPERTS)),
        'moe_w1': nrm(ks[23], (DEPTH, N_EXPERTS, D, EXPERT_HIDDEN), D),
        'moe_w3': nrm(ks[24], (DEPTH, N_EXPERTS, D, EXPERT_HIDDEN), D),
        'moe_w2': nrm(ks[25], (DEPTH, N_EXPERTS, EXPERT_HIDDEN, D), EXPERT_HIDDEN),
    }

def reference(x, c, ada_w, ada_b, norm_mix, norm_ffn, ret_w_in, ret_gn, ret_w_out,
              kv_ada_w, kv_ada_b, kv_norm, kv_w, k_norm, diff_w_q, q_norm, diff_lam,
              diff_subln, diff_w_out, moe_w_group, moe_b_group, moe_w_expert, moe_b_expert,
              moe_w1, moe_w3, moe_w2):
    c_act = jax.nn.silu(c)
    k_shared = None
    v_shared = None
    for layer in range(DEPTH):
        sh1, sc1, g1, sh2, sc2, g2 = jnp.split(c_act @ ada_w[layer] + ada_b[layer], 6, axis=-1)
        h = _modulate(_rmsnorm(x, norm_mix[layer]), sh1, sc1)
        if layer < N_A_LAYERS:
            a = layer
            y = _retention(h, ret_w_in[a], ret_gn[a], ret_w_out[a])
        else:
            b = layer - N_A_LAYERS
            if b == 0:
                k_shared, v_shared = _shared_kv(x, c_act, kv_ada_w, kv_ada_b, kv_norm, kv_w, k_norm)
            lambda_init = 0.8 - 0.6 * math.exp(-0.3 * layer)
            y = _diff_attention(h, k_shared, v_shared, diff_w_q[b], q_norm[b], diff_lam[b],
                                diff_subln[b], diff_w_out[b], lambda_init)
        x = x + g1[:, None, :] * y
        h = _modulate(_rmsnorm(x, norm_ffn[layer]), sh2, sc2)
        x = x + g2[:, None, :] * _hier_moe(h, moe_w_group[layer], moe_b_group[layer],
                                           moe_w_expert[layer], moe_b_expert[layer],
                                           moe_w1[layer], moe_w3[layer], moe_w2[layer])
    return x


_drawn_inputs = setup_inputs


def setup_inputs(seed=0):
    import zlib

    import numpy as np

    out = dict(_drawn_inputs(seed))
    spreads = {}
    factors = {'kv_ada_b': 3.821,
     'kv_norm': 6.432,
     'k_norm': 6.265,
     'q_norm': 8.0,
     'diff_lam': 2.876,
     'diff_subln': 4.726,
     'moe_b_group': 3.62,
     'moe_b_expert': 3.964}
    for name, (base, spread) in spreads.items():
        noise = np.random.default_rng([zlib.crc32(name.encode()), seed]).standard_normal(out[name].shape)
        drawn = base * np.exp(spread * noise) if base else spread * noise
        out[name] = jnp.asarray(drawn.astype(out[name].dtype))
    for name, factor in factors.items():
        out[name] = (out[name] * factor).astype(out[name].dtype)
    return out
```

```python
import math
from contextlib import ExitStack

import numpy as np

import concourse.bass as bass
from concourse import mybir
from concourse.alu_op_type import AluOpType as ALU

F32 = mybir.dt.float32
F32R = mybir.dt.float32r
I32 = mybir.dt.int32
ACT = mybir.ActivationFunctionType
AX = mybir.AxisListType
ds = bass.ds

P = 128
T = 512
D = 1024
TT = T // P
KD = D // P
EPS = 1e-6
RH, RK, RV = 4, 256, 512
AHEADS, HD = 8, 64
LAMBDA_INIT = 0.8 - 0.6 * math.exp(-0.3)
CHUNK = 64
NG, EPG = 4, 4
NE = NG * EPG
MAX_OVER = (2 * T) // (P + 1)
Y_BLOCKS = NE + 2 * RH
assert Y_BLOCKS >= NE + MAX_OVER
BIG = 1e30

RING = 4
PRE_CHUNKS = 8
HEAD_CHUNKS, HEAD_SPLIT = 20, 8
MOE_CHUNKS = 12
MIX_CHUNKS = 16
HALVES = 28
HEAD_ORDER = [0, "a", "a", 1, "a", "a", 2, "a", "a", 3, "a", "a", 4, "a", "a", 5, "a", "a", 6, 7]
KV_SLOT = [0, 1, 2, 0, 1, 2, 0, 1]
HALF_SLOT = [2, 0, 1, 0]


def shape_constants():
    table = np.zeros((P, 3 * P), np.float32)
    table[:, 0:P] = np.eye(P)
    table[:, P:2 * P] = np.triu(np.ones((P, P)), 1)
    table[:, 2 * P:3 * P] = np.arange(P)[None, :]
    half = RK // 2
    inv = (1.0 / (np.float32(10000.0) ** (np.arange(half, dtype=np.float32) / np.float32(half)))).astype(np.float32)
    ang = (np.arange(T, dtype=np.float32)[:, None] * inv[None, :]).astype(np.float32)
    rope = np.stack([np.cos(ang), np.sin(ang)]).astype(np.float32)
    decay = np.zeros((RH, P, T), np.float64)
    log_gamma = np.log1p(-np.exp2(-5.0 - np.arange(RH)))
    rel = np.arange(T)[None, :] - np.arange(P)[:, None]
    for h in range(RH):
        decay[h] = np.where(rel >= 0, np.exp(rel * log_gamma[h]), 0.0) * RK ** -0.5
    return {"table": table, "rope": rope, "decay": decay.astype(np.float32)}


def build_trunk(nc, io, out):
    ctx = ExitStack()

    def sb(name, shape, dt=F32):
        return ctx.enter_context(nc.sbuf_tensor(name, shape, dt))

    def sem(name):
        return ctx.enter_context(nc.semaphore(name))

    with ctx:
        AH = sb("act_hi", [P, KD, T], F32R)
        AL = sb("act_lo", [P, KD, T], F32R)
        BH = sb("act2_hi", [P, 2048], F32R)
        BL = sb("act2_lo", [P, 2048], F32R)
        WH = sb("w_hi", [P, RING, 2048], F32R)
        WL = sb("w_lo", [P, RING, 2048], F32R)
        PT = sb("pick", [P, TT, P], F32R)
        RAW = sb("w_raw", [P, RING, 2048])
        X = sb("x_res", [P, TT, D])
        TAB = sb("table", [P, 3 * P])
        ONES = sb("ones", [P, 2])
        SM = sb("small", [P, 96])
        SC = sb("scratch", [P, 11200])
        NBI = sb("n_over_i", [1, 2], I32)
        OEI = sb("over_expert_i", [1, 8], I32)
        DESTI = sb("dest_i", [P, 2 * TT], I32)
        ident, tri, iota = TAB[:, 0:P], TAB[:, P:2 * P], TAB[:, 2 * P:3 * P]
        cT, eps, ss, rstd = SM[:, 0:8], SM[:, 8:9], SM[:, 9:13], SM[:, 13:17]
        qn, kn_g, subln, nlam = SM[:, 17:18], SM[:, 18:19], SM[:, 19:20], SM[:, 20:21]
        credit = SM[:, 21:22]
        st8a, st8b = SM[:, 24:40], SM[:, 40:56]
        att = SM[:, 56:72]
        sdv = SM[:, 72:76]
        so, sd_o = SM[:, 76:80], SM[:, 80:84]
        lam_s = SM[:, 84:88]

        def sc(at, n):
            return SC[:, at:at + n]

        qkT = sc(0, 2048).rearrange("p (j t) -> p j t", j=4)
        V1 = sc(2048, 2048).rearrange("p (t v) -> p t v", t=TT)
        QKR = sc(4096, 1024).rearrange("p (b n) -> p b n", b=2)
        SG = sc(4096, 1024).rearrange("p (b n) -> p b n", b=2)
        ST = sc(5120, 1280)
        ROT = sc(5120, 1024).rearrange("p (b n) -> p b n", b=2)
        TMP = sc(5120, 1024).rearrange("p (b n) -> p b n", b=2)
        DEC, GN, ACC1, ROW = sc(6400, 512), sc(6912, 512), sc(7424, 512), SC[0:1, 7936:8448]
        GATE = sc(8448, 1024)
        ROPE = sc(9472, 1024).rearrange("p (s t d) -> p s t d", s=2, t=TT)

        ACC = ctx.enter_context(nc.psum_tensor("acc", [P, 4, 512], F32))
        AUX = ctx.enter_context(nc.psum_tensor("aux", [P, 4, 512], F32))

        ada_rows = nc.dram_tensor("ada_rows", (HALVES, 512), F32, kind="Internal").ap()
        y_rows = nc.dram_tensor("y_rows", (Y_BLOCKS * P, D), F32, kind="Internal").ap()

        raw_arrived = [sem(f"raw_arrived{s}") for s in range(RING)]
        raw_used = sem("raw_used")
        hi_done = sem("hi_done")
        pe_steps = sem("pe_steps")
        started = sem("started")
        table_in, rope_in, cols_in = sem("table_in"), sem("rope_in"), sem("cols_in")
        x_in = sem("x_in")
        c_in = sem("c_in")
        cact_done = sem("cact_done")
        bias_in = sem("bias_in")
        row_ready = sem("row_ready")
        row_out = sem("row_out")
        ada_ready = sem("ada_ready")
        ada_ps = sem("ada_ps")
        mod_in = sem("mod_in")
        mod_free = sem("mod_free")
        n_sd, n_rows, n_T, n_hi, n_lo = (sem(x) for x in ("n_sd", "n_rows", "n_T", "n_hi", "n_lo"))
        gate_in = sem("gate_in")
        gate_free = sem("gate_free")
        head_in = sem("head_in")
        acc_free = sem("acc_free")
        rot_done, qk_T, qk_out = sem("rot_done"), sem("qk_T"), sem("qk_out")
        st_ps, st_done = sem("st_ps"), sem("st_done")
        pv_ps, o_sd, o_norm = sem("pv_ps"), sem("o_sd"), sem("o_norm")
        silu_done, y_done, y_T, y_hi, y_lo = (sem(x) for x in ("silu_done", "y_done", "y_T", "y_hi", "y_lo"))
        x_done = sem("x_done")
        out_done = sem("out_done")
        ht_out, lg_ps, lg_exp, lg_in = sem("ht_out"), sem("lg_ps"), sem("lg_exp"), sem("lg_in")
        cnt_ready, rank_ps = sem("cnt_ready"), sem("rank_ps")
        routed, over_set, pick_ready, picked = sem("routed"), sem("over_set"), sem("pick_ready"), sem("picked")
        xt_hi, xt_lo = sem("xt_hi"), sem("xt_lo")
        act_g, hid_done, hid_T, hid_hi, hid_lo = (sem(x) for x in ("act_g", "hid_done", "hid_T", "hid_hi", "hid_lo"))
        pool_held = sem("pool_held")
        sp_held = sem("sp_held")
        zero_set = sem("zero_set")
        y_half_a, y_half_v = sem("y_half_a"), sem("y_half_v")
        y_store = sem("y_store")
        back_in = [sem("back_in0"), sem("back_in1")]
        back_used, back_act = sem("back_used"), sem("back_act")
        a_sq, a_ss, a_sd, a_kn, a_T, a_kv = (sem(x) for x in ("a_sq", "a_ss", "a_sd", "a_kn", "a_T", "a_kv"))
        ks_in, s_ps, s_max, s_exp, s_a, s_aT, s_at = (sem(x) for x in ("ks_in", "s_ps", "s_max", "s_exp", "s_a", "s_aT", "s_at"))
        s_o, s_so, s_on, s_oT, s_ohi, s_olo = (sem(x) for x in ("s_o", "s_so", "s_on", "s_oT", "s_ohi", "s_olo"))
        lam_in, lam_sum, lam_exp, lam_ready = sem("lam_in"), sem("lam_sum"), sem("lam_exp"), sem("lam_ready")
        own = {e: sem(f"own_{e}") for e in ("act", "dve", "pool")}

        def hold(pool, s, value):
            pool.wait_ge(s, value)
            pool.sem_inc(pool_held, 1)

        class Own:

            def __init__(self, eng, name):
                self.eng, self.sem, self.base, self.n = eng, own[name], 0, 0
                self.pool = name == "pool"

            def step(self, ins):
                self.n += 1
                ins.then_inc(self.sem, 1)
                self.eng.wait_ge(self.sem, self.base + self.n)
                if self.pool:
                    self.eng.sem_inc(pool_held, 1)

            def enter(self, i, per):
                self.saved = (self.base + self.n, per)
                self.base, self.n = i * per + self.saved[0], 0

            def leave(self, times):
                at, per = self.saved
                assert self.n == per, (self.n, per)
                self.base, self.n = at + times * per if not isinstance(times, int) else at + times * per, 0

        C_HEAD = PRE_CHUNKS
        C_MOE0 = C_HEAD + RH * HEAD_CHUNKS
        S_MOE0 = RH * HEAD_SPLIT

        def moe_c(layer, n0):
            return C_MOE0 if layer == 0 else n0 * MOE_CHUNKS + (C_MOE0 + MIX_CHUNKS)

        def moe_s(layer, n0):
            return S_MOE0 if layer == 0 else n0 * MOE_CHUNKS + (S_MOE0 + MIX_CHUNKS)

        def moe_arrived(layer, n0, slot):
            at = C_MOE0 // RING
            return at if layer == 0 else n0 * (MOE_CHUNKS // RING) + (at + [7, 5, 4, 0][slot])

        def load_chunk(eng, slot, src, kt, used):
            if used is not None:
                eng.wait_ge(raw_used, used)
                eng.sem_inc(sp_held, 1)
            eng.dma_start(RAW[:, slot, :].rearrange("p (k n) -> p k n", k=kt), src).then_inc(raw_arrived[slot], 16)

        def split_hi(eng, rslot, wslot, arrived, steps):
            eng.wait_ge(raw_arrived[rslot], 16 * arrived)
            if steps is not None:
                eng.wait_ge(pe_steps, steps)
            eng.activation(WH[:, wslot, :], RAW[:, rslot, :], ACT.Copy).then_inc(hi_done, 1)

        def split_lo(eng, rslot, wslot, arrived, steps, hi):
            eng.wait_ge(raw_arrived[rslot], 16 * arrived)
            if steps is not None:
                eng.wait_ge(pe_steps, steps)
            eng.wait_ge(hi_done, hi)
            eng.tensor_tensor(WL[:, wslot, :], RAW[:, rslot, :], WH[:, wslot, :].bitcast(F32),
                              ALU.subtract).then_inc(raw_used, 1)

        def mm3(out_ap, ah, al, wh, wl, first, last):
            nc.tensor.matmul(out_ap, ah, wh, start=first, stop=False)
            nc.tensor.matmul(out_ap, ah, wl, start=False, stop=False)
            return nc.tensor.matmul(out_ap, al, wh, start=False, stop=last)


        def norm_views(n):
            if n in (0, 1, 4):
                return dict(HR=sc(0, 2048), S=sc(2048, 1024), B=sc(3072, 1024), G=sc(4096, 1024),
                            J=sc(5120, 1024) if n == 0 else sc(6400, 1024))
            if n == 2:
                return dict(HR=sc(8192, 2048), S=sc(0, 1024), B=sc(1024, 1024), G=sc(2048, 1024), J=sc(4096, 1024))
            return dict(HR=sc(8192, 2048), S=RAW[:, 3, 0:1024], B=RAW[:, 3, 1024:2048], G=sc(9216, 1024))

        NORM_ROWS = [0, 3, 6, 8, 11]
        NORM_GAIN = [io["norm_mix"][0:1, :], io["norm_ffn"][0:1, :], io["kv_norm"].rearrange("(a n) -> a n", a=1),
                     io["norm_mix"][1:2, :], io["norm_ffn"][1:2, :]]
        rows2 = ada_rows.rearrange("(v h) n -> v (h n)", h=2)
        X_DONE = {1: 32, 2: 36, 3: 36, 4: 52, 5: 56}
        SD_BASE = {0: 0, 1: 4, 2: 8, 4: 12}

        def norm_pool(pool, n):
            v = norm_views(n)
            pool.dma_start(v["B"], rows2[NORM_ROWS[n]:NORM_ROWS[n] + 1, :].broadcast_to([P, D])).then_inc(mod_in, 16)
            pool.dma_start(v["S"], rows2[NORM_ROWS[n] + 1:NORM_ROWS[n] + 2, :].broadcast_to([P, D])).then_inc(mod_in, 16)
            pool.dma_start(v["G"], NORM_GAIN[n].broadcast_to([P, D])).then_inc(mod_in, 16)

        def norm_act_stats(act, n, o):
            v = norm_views(n)
            for t in range(TT):
                if n == 0:
                    act.wait_ge(x_in, 16)
                else:
                    act.wait_ge(x_done, X_DONE[n] - TT + t + 1)
                o.step(act.activation(v["J"], X[:, t, :], ACT.Square, accum_out=ss[:, t:t + 1]))
                act.activation(sdv[:, t:t + 1], ss[:, t:t + 1], ACT.Sqrt, bias=eps, scale=1.0 / D).then_inc(n_sd, 1)

        def norm_dve_rows(dve, n, t, o):
            v = norm_views(n)
            if t == 0:
                dve.wait_ge(mod_in, 48 * (n + 1))
                o.step(dve.scalar_tensor_tensor(v["S"], v["S"], 1.0, v["G"], ALU.add, ALU.mult))
            if n != 3:
                dve.wait_ge(n_sd, SD_BASE[n] + t + 1)
                o.step(dve.reciprocal(rstd[:, t:t + 1], sdv[:, t:t + 1]))
            hr = v["HR"][:, (t % 2) * D:(t % 2 + 1) * D]
            if t >= 2:
                dve.wait_ge(n_T, TT * n + t - 1)
            o.step(dve.scalar_tensor_tensor(hr, X[:, t, :], rstd[:, t:t + 1], v["S"], ALU.mult, ALU.mult))
            dve.tensor_tensor(hr, hr, v["B"], ALU.add).then_inc(n_rows, 1)

        def norm_pe(pe, n, t):
            hr = norm_views(n)["HR"][:, (t % 2) * D:(t % 2 + 1) * D]
            pe.wait_ge(n_rows, TT * n + t + 1)
            if t >= 2:
                if n in (1, 4):
                    pe.wait_ge(ht_out, TT * (n == 4) + t - 1)
                else:
                    pe.wait_ge(n_lo, TT * n + t - 1)
            for k in range(KD):
                q = 2 * (t % 2) + k // 4
                last = nc.tensor.transpose(AUX[:, q, (k % 4) * P:(k % 4 + 1) * P], hr[:, k * P:(k + 1) * P], ident)
            last.then_inc(n_T, 1)

        def aux_pair(t):
            return AUX[:, 2 * (t % 2):2 * (t % 2) + 2, :].rearrange("p a (k c) -> p (a k) c", c=P)

        def norm_act_hi(act, n):
            for t in range(TT):
                act.wait_ge(n_T, TT * n + t + 1)
                act.activation(AH[:, :, t * P:(t + 1) * P], aux_pair(t), ACT.Copy).then_inc(n_hi, 1)

        def norm_dve_lo(dve, n, t):
            dve.wait_ge(n_hi, TT * n + t + 1)
            dve.tensor_tensor(AL[:, :, t * P:(t + 1) * P], aux_pair(t), AH[:, :, t * P:(t + 1) * P].bitcast(F32),
                              ALU.subtract).then_inc(n_lo, 1)

        def norm_dve(dve, n, o):
            for t in range(TT):
                norm_dve_rows(dve, n, t, o)
                if t:
                    norm_dve_lo(dve, n, t - 1)
            norm_dve_lo(dve, n, TT - 1)

        def ada_acc(dve, o, q, slots, arrived):
            for m in range(2):
                dve.wait_ge(raw_arrived[slots[m]], arrived[m] * 16)
                for k in range(4):
                    w = RAW[:, slots[m], k * 512:(k + 1) * 512]
                    s = cT[:, 4 * m + k:4 * m + k + 1]
                    if m == 0 and k == 0:
                        dve.wait_ge(ada_ps, q)
                        o.step(dve.tensor_scalar(ACC1, w, s, None, ALU.mult))
                    else:
                        o.step(dve.scalar_tensor_tensor(ACC1, w, s, ACC1, ALU.mult, ALU.add))
                dve.sem_inc(raw_used, 1)
            dve.sem_inc(ada_ready, 1)

        def ada_sum(pe, q):
            pe.wait_ge(ada_ready, q + 1)
            pe.wait_ge(row_ready, q)
            nc.tensor.matmul(AUX[0:1, 3, :], ONES[:, 0:1], ACC1, start=True, stop=True).then_inc(ada_ps, 1)

        def ada_row(dve, q):
            dve.wait_ge(ada_ps, q + 1)
            dve.wait_ge(bias_in, (q + 1) * 16)
            dve.tensor_tensor(ROW, AUX[0:1, 3, :], ROW, ALU.add).then_inc(row_ready, 1)

        def ada_store(pool, q, bias, flat):
            hold(pool, row_out, q * 16)
            pool.dma_start(ROW, bias).then_inc(bias_in, 16)
            hold(pool, row_ready, q + 1)
            pool.dma_start(ada_rows[flat, :], ROW).then_inc(row_out, 16)

        def head_half(h, j):
            if j < 2:
                col, flat = h * 1024 + (2048 + 512 * j), h * 2 + (4 + j)
                return io["ada_w"][0:1, :, ds(col, 512)], io["ada_b"][0:1, ds(col, 512)], ds(flat, 1)
            if j == 2:
                return (io["kv_ada_w"].rearrange("(o k) n -> o k n", o=1)[:, :, ds(h * 512, 512)],
                        io["kv_ada_b"].rearrange("(o n) -> o n", o=1)[:, ds(h * 512, 512)], ds(h + 12, 1))
            col = h * 1536 + 512 * (j - 3)
            return io["ada_w"][1:2, :, ds(col, 512)], io["ada_b"][1:2, ds(col, 512)], ds(h * 3 + (16 + j - 3), 1)

        def k_rows(w, kt, q):
            return w[:, q * kt * P:(q + 1) * kt * P, :].rearrange("o (k p) n -> p (o k) n", p=P)

        def head_pos(h, i):
            return (h * HEAD_CHUNKS + (C_HEAD + i), i % RING, h * (HEAD_CHUNKS // RING) + (C_HEAD // RING + i // RING + 1))

        def free_steps(S):
            return S * 4 + 4

        def fin(S, t=3):
            return S * 4 + (17 + t)

        AT_SPLIT = [HEAD_ORDER.index(x) for x in range(8)]
        AT_ADA = [[i for i, x in enumerate(HEAD_ORDER) if x == "a"][2 * j:2 * j + 2] for j in range(6)]

        def project(pe, S0, C0s, w, ah, al, between=None, halves=1):
            for q in range(2):
                pe.wait_ge(raw_used, C0s[q] + 5)
                slot = (S0[1] + q) % RING
                for t in range(TT):
                    if q == 0:
                        pe.wait_ge(acc_free, w * 4 + (t + 1))
                    if halves == 2:
                        o, ks, n = ACC[:, t, q * 256:(q + 1) * 256], range(KD), 256
                    else:
                        o, ks, n = ACC[:, t, :], range(4), 512
                    for k in ks:
                        kt = k if halves == 2 else 4 * q + k
                        last = mm3(o, ah(kt, t), al(kt, t), WH[:, slot, k * n:(k + 1) * n], WL[:, slot, k * n:(k + 1) * n],
                                   first=(k == 0 and (q == 0 or halves == 2)),
                                   last=(k == ks[-1] and (q == 1 or halves == 2)))
                    last.then_inc(pe_steps, 1)
                    if between:
                        between(q, t)

        def out_project(pe, S0, C0, w, q, ready):
            pe.wait_ge(raw_used, C0 + 5)
            for t in range(TT):
                if ready:
                    ready(t)
                pe.wait_ge(acc_free, w * 4 + (t + 1))
                for k in range(4):
                    lhs = slice(k * T + t * P, k * T + (t + 1) * P)
                    last = mm3(ACC[:, t, :], BH[:, lhs], BL[:, lhs], WH[:, S0 % RING, k * 512:(k + 1) * 512],
                               WL[:, S0 % RING, k * 512:(k + 1) * 512], first=(k == 0), last=(k == 3))
                last.then_inc(pe_steps, 1)

        def hT(A):
            return lambda kt, t: A[:, kt, t * P:(t + 1) * P]

        XTH, HTH = BH[:, 0:1024], BH[:, 1024:2048]
        XTL, HTL = BL[:, 0:1024], BL[:, 1024:2048]
        SIL, HID, YS = sc(0, 1024), sc(1024, 1024), sc(2048, 1024)
        rows_hi = AH[:, :, :].rearrange("p a b -> p (a b)").rearrange("p (t d) -> p t d", t=TT)
        rows_lo = AL[:, :, :].rearrange("p a b -> p (a b)").rearrange("p (t d) -> p t d", t=TT)
        W_NAME = ["moe_w1", "moe_w3", "moe_w2"]

        def expert_load(sp, layer, c0, b, expert, first):
            for m in range(MOE_CHUNKS):
                src = io[W_NAME[m // 4]][layer:layer + 1, ds(expert, 1), (m % 4) * 256:(m % 4 + 1) * 256, :]
                used = b * MOE_CHUNKS + c0 + (m + 1)
                if first and layer == 1 and m < RING:
                    used = c0 + 4
                load_chunk(sp, m % RING, src.rearrange("o e (k p) n -> p (o e k) n", p=P), 2, used)

        def pick_tokens(pe, g, part):
            rows = (rows_hi, rows_lo)[part]
            if part == 0:
                pe.wait_ge(pick_ready, g + 1)
            for k in range(KD):
                for t in range(TT):
                    last = nc.tensor.matmul(AUX[:, 2 * part + k // 4, (k % 4) * P:(k % 4 + 1) * P],
                                            rows[:, t, k * P:(k + 1) * P], PT[:, t, :], start=(t == 0), stop=(t == TT - 1))
            if part == 1:
                last.then_inc(picked, 1)

        def expert_pe(pe, layer, c0, s0, b, B):
            g = B + layer
            def mms(m, x_hi, x_lo, bank):
                pe.wait_ge(raw_used, b * MOE_CHUNKS + c0 + (m + 5))
                for k in range(2):
                    kt = 2 * (m % 4) + k
                    for n in range(2):
                        at = k * 1024 + n * 512
                        last = mm3(ACC[:, bank + n, :], x_hi[:, kt * P:(kt + 1) * P], x_lo[:, kt * P:(kt + 1) * P],
                                   WH[:, m % RING, at:at + 512], WL[:, m % RING, at:at + 512],
                                   first=(kt == 0), last=(kt == KD - 1))
                last.then_inc(pe_steps, 4)
            pe.wait_ge(xt_hi, g + 1)
            pe.wait_ge(xt_lo, g + 1)
            if not isinstance(B, int):
                pe.wait_ge(y_half_a, B)
                pe.wait_ge(y_half_v, B)
            for m in range(8):
                mms(m, XTH, XTL, 2 * (m // 4))
            pick_tokens(pe, g + 1, 0)
            pe.wait_ge(hid_done, B + 1)
            for k in range(KD):
                last = nc.tensor.transpose(ACC[:, 2 + k // 4, (k % 4) * P:(k % 4 + 1) * P], HID[:, k * P:(k + 1) * P], ident)
            last.then_inc(hid_T, 1)
            pick_tokens(pe, g + 1, 1)
            pe.wait_ge(hid_hi, B + 1)
            pe.wait_ge(hid_lo, B + 1)
            for m in range(8, 12):
                mms(m, HTH, HTL, 0)

        up_pair = ACC[:, 2:4, :].rearrange("p a n -> p (a n)")
        gate_pair = ACC[:, 0:2, :].rearrange("p a n -> p (a n)")

        def y_out_act(act, s_last, B_done):
            act.wait_ge(pe_steps, fin(s_last))
            act.wait_ge(y_store, B_done * 16 + 16 * RH)
            act.activation(YS[:, 0:512], ACC[:, 0, :], ACT.Copy).then_inc(y_half_a, 1)

        def y_out_dve(dve, s_last, B_done):
            dve.wait_ge(pe_steps, fin(s_last))
            dve.wait_ge(y_store, B_done * 16 + 16 * RH)
            dve.tensor_copy(YS[:, 512:1024], ACC[:, 1, :]).then_inc(y_half_v, 1)

        def y_out_pool(pool, layer, b_last, B_done):
            hold(pool, y_half_a, B_done + 1)
            hold(pool, y_half_v, B_done + 1)
            pool.dma_start(y_rows[ds(b_last * P, P), :], YS).then_inc(y_store, 16)

        def tokens_hi(act, g):
            act.wait_ge(picked, g + 1)
            act.activation(XTH, AUX[:, 0:2, :].rearrange("p a n -> p (a n)"), ACT.Copy).then_inc(xt_hi, 1)

        def tokens_lo(dve, g):
            dve.wait_ge(picked, g + 1)
            dve.tensor_copy(XTL, AUX[:, 2:4, :].rearrange("p a n -> p (a n)")).then_inc(xt_lo, 1)

        def expert_act(act, layer, n0, s0, b, B, first):
            def hi(m):
                split_hi(act, m % RING, m % RING, b * 3 + moe_arrived(layer, n0, m % RING) + (m // RING + 1),
                         free_steps(b * MOE_CHUNKS + s0 + m))
            for m in range(3):
                hi(m)
            if not first:
                y_out_act(act, b * MOE_CHUNKS + s0 - 1, B - 1)
            for m in range(3, 7):
                hi(m)
            act.wait_ge(pe_steps, fin(b * MOE_CHUNKS + s0 + 3))
            act.activation(SIL, gate_pair, ACT.Silu).then_inc(act_g, 1)
            for m in range(7, 12):
                hi(m)
            act.wait_ge(hid_T, B + 1)
            act.activation(HTH, up_pair, ACT.Copy).then_inc(hid_hi, 1)
            tokens_hi(act, B + (layer + 1))

        def expert_dve(dve, layer, n0, c0, s0, b, B, first):
            def lo(m):
                split_lo(dve, m % RING, m % RING, b * 3 + moe_arrived(layer, n0, m % RING) + (m // RING + 1),
                         free_steps(b * MOE_CHUNKS + s0 + m), b * MOE_CHUNKS + s0 + (m + 1))
            for m in range(3):
                lo(m)
            if not first:
                y_out_dve(dve, b * MOE_CHUNKS + s0 - 1, B - 1)
            for m in range(3, 11):
                lo(m)
            dve.wait_ge(pe_steps, fin(b * MOE_CHUNKS + s0 + 7))
            dve.wait_ge(act_g, B + 1)
            dve.tensor_tensor(HID, up_pair, SIL, ALU.mult).then_inc(hid_done, 1)
            lo(11)
            dve.wait_ge(hid_hi, B + 1)
            dve.tensor_tensor(HTL, up_pair, HTH.bitcast(F32), ALU.subtract).then_inc(hid_lo, 1)
            tokens_lo(dve, B + (layer + 1))

        R0 = 9472
        at = [R0]

        def small(n, inner=None):
            v = SC[:, at[0]:at[0] + n]
            at[0] += n
            return v if inner is None else v.rearrange("p (a b) -> p a b", b=inner)

        LG, EX, EXR = small(80, 20), small(20), small(20)
        GM, GS, GT, BEST, M1, M2, WB = (small(4) for _ in range(7))
        RV4, RV16, E128, ADJ, OB, OST = small(4), small(16), small(16), small(16), small(16), small(16)
        GA, OG = small(16, 4), small(16, 4)
        EL, EA, O1, O2, CN, DS1 = (small(64, 16) for _ in range(6))
        CS = [small(24), small(24)]
        WTS, DEST, DD = small(8, 4), small(8, 4), small(8, 4)
        OVX, OVE = small(8 * 16, 16), small(8)
        BR = small(20)
        assert at[0] <= 10240 + 200, at
        WR = sc(7424, 160).rearrange("p (k n) -> p k n", n=20)
        HTF = sc(5120, 1024).rearrange("p (k c) -> p k c", c=P)
        PICKA, PICKB = sc(10500, 128), sc(10628, 512)

        def col(v, n):
            return v.rearrange("p (a o) -> p a o", o=1).broadcast_to([P, v.shape[1], n])

        def row(v, a, parts=P):
            return v.rearrange("p (o n) -> p o n", o=1).broadcast_to([parts, a, v.shape[1]])

        def moe_norm_act(act, n, o):
            layer = int(n == 4)
            norm_act_stats(act, n, o)
            for t in range(TT):
                act.wait_ge(n_rows, TT * n + t + 1)
                hr = norm_views(n)["HR"][:, (t % 2) * D:(t % 2 + 1) * D]
                act.activation(rows_hi[:, t, :], hr, ACT.Copy).then_inc(n_hi, 1)
                act.wait_ge(n_T, TT * n + t + 1)
                act.wait_ge(lg_ps, TT * layer + t)
                act.activation(HTF, aux_pair(t), ACT.Copy).then_inc(ht_out, 1)

        def moe_norm_dve(dve, n, o):
            def lo(t):
                dve.wait_ge(n_hi, TT * n + t + 1)
                hr = norm_views(n)["HR"][:, (t % 2) * D:(t % 2 + 1) * D]
                o.step(dve.tensor_tensor(rows_lo[:, t, :], hr, rows_hi[:, t, :].bitcast(F32), ALU.subtract))
                dve.sem_inc(n_lo, 1)
            for t in range(TT):
                norm_dve_rows(dve, n, t, o)
                if t:
                    lo(t - 1)
            lo(TT - 1)

        def moe_norm_pe(pe, n):
            layer = int(n == 4)
            def logits(t):
                pe.wait_ge(ht_out, TT * layer + t + 1)
                if t == 0:
                    pe.wait_ge(lg_in, 64 * (layer + 1))
                for k in range(KD):
                    last = nc.tensor.matmul(ACC[:, 3, t * 20:(t + 1) * 20], HTF[:, k, :], WR[:, k, :],
                                            start=(k == 0), stop=(k == KD - 1))
                last.then_inc(lg_ps, 1)
            norm_pe(pe, n, 0)
            for t in range(1, TT):
                norm_pe(pe, n, t)
                logits(t - 1)
            logits(TT - 1)

        def route_dve(dve, layer, o):
            st = o.step
            st(dve.tensor_scalar(RV4, iota[:, 0:NG], -1.0, float(NG), ALU.mult, ALU.add))
            st(dve.tensor_scalar(RV16, iota[:, 0:NE], -1.0, float(NE), ALU.mult, ALU.add))
            st(dve.tensor_scalar(E128, iota[:, 0:NE], float(P), None, ALU.mult))
            st(dve.memset(CS[0], 0.0))
            st(dve.memset(CS[1], 0.0))
            dve.wait_ge(lg_ps, TT * (layer + 1))
            st(dve.tensor_tensor(LG, ACC[:, 3, 0:80].rearrange("p (t n) -> p t n", n=20), row(BR, TT), ALU.add))
            gl, el = LG[:, :, 0:NG], LG[:, :, NG:20]
            st(dve.tensor_reduce(GM, gl, AX.X, ALU.max))
            exg = EX[:, 0:16].rearrange("p (a b) -> p a b", b=4)
            st(dve.tensor_tensor(exg, gl, col(GM, NG), ALU.subtract))
            st(dve.tensor_tensor(GA, gl, col(GM, NG), ALU.is_equal))
            st(dve.tensor_tensor(GA, GA, row(RV4, TT), ALU.mult))
            st(dve.tensor_reduce(BEST, GA, AX.X, ALU.max))
            st(dve.tensor_tensor(OG, row(RV4, TT), col(BEST, NG), ALU.is_equal))
            st(dve.tensor_scalar(OG, OG, -1.0, BIG, ALU.add, ALU.mult))
            og4 = OG.rearrange("p t (g o) -> p t g o", o=1).broadcast_to([P, TT, NG, EPG])
            st(dve.tensor_tensor(EL.rearrange("p t (g e) -> p t g e", e=EPG), el.rearrange("p t (g e) -> p t g e", e=EPG),
                                 og4, ALU.add))

            def top(m, one):
                st(dve.tensor_reduce(m, EL, AX.X, ALU.max))
                st(dve.tensor_tensor(EA, EL, col(m, NE), ALU.is_equal))
                st(dve.tensor_tensor(EA, EA, row(RV16, TT), ALU.mult))
                st(dve.tensor_reduce(BEST, EA, AX.X, ALU.max))
                st(dve.tensor_tensor(one, row(RV16, TT), col(BEST, NE), ALU.is_equal))
            top(M1, O1)
            st(dve.scalar_tensor_tensor(EL, O1, -3.0 * BIG, EL, ALU.mult, ALU.add))
            top(M2, O2)
            st(dve.tensor_tensor(EX[:, 16:20], M2, M1, ALU.subtract))
            st(dve.tensor_tensor(CN, O1, O2, ALU.add))
            dve.sem_inc(cnt_ready, 1)
            dve.wait_ge(lg_exp, layer + 1)
            st(dve.tensor_reduce(GS, EXR[:, 0:16].rearrange("p (a b) -> p a b", b=4), AX.X, ALU.add))
            st(dve.tensor_scalar(WB, EXR[:, 16:20], 1.0, None, ALU.add))
            st(dve.tensor_tensor(GT, GS, WB, ALU.mult))
            st(dve.reciprocal(WTS[:, 0, :], GT))
            st(dve.tensor_tensor(WTS[:, 1, :], WTS[:, 0, :], EXR[:, 16:20], ALU.mult))
            dve.wait_ge(rank_ps, layer + 1)
            tot = AUX[:, 1, 0:NE]
            st(dve.tensor_scalar(OB, tot, float(P), None, ALU.is_gt))
            st(dve.scalar_tensor_tensor(OB, tot, 2.0 * P, OB, ALU.is_gt, ALU.add))
            st(dve.scalar_tensor_tensor(OB, tot, 3.0 * P, OB, ALU.is_gt, ALU.add))
            st(dve.tensor_copy(CS[0][:, 8:24], OB))
            for i, s in enumerate((1, 2, 4, 8)):
                a, b = CS[i % 2], CS[1 - i % 2]
                st(dve.tensor_tensor(b[:, 8:24], a[:, 8:24], a[:, 8 - s:24 - s], ALU.add))
            oend = CS[0][:, 8:24]
            st(dve.tensor_tensor(OST, oend, OB, ALU.subtract))
            st(dve.tensor_copy(NBI[0:1, layer:layer + 1], oend[0:1, 15:16]))
            ov = OVX[0:1, 0:MAX_OVER, :]
            it = iota[0:1, 0:MAX_OVER].rearrange("p (a o) -> p a o", o=1).broadcast_to([1, MAX_OVER, NE])
            st(dve.tensor_tensor(ov, row(oend[0:1, :], MAX_OVER, 1), it, ALU.is_le))
            st(dve.tensor_reduce(OVE[0:1, 0:MAX_OVER], ov, AX.X, ALU.add))
            st(dve.tensor_scalar(OVE[0:1, 0:MAX_OVER], OVE[0:1, 0:MAX_OVER], float(NE - 1), None, ALU.min))
            st(dve.tensor_copy(OEI[0:1, 0:MAX_OVER], OVE[0:1, 0:MAX_OVER]))
            dve.sem_inc(over_set, 1)
            rank = AUX[:, 0, 0:64].rearrange("p (t e) -> p t e", e=NE)
            st(dve.scalar_tensor_tensor(ADJ, OST, float(P), E128, ALU.mult, ALU.subtract))
            st(dve.tensor_scalar(ADJ, ADJ, float((NE - 1) * P), None, ALU.add))
            st(dve.tensor_scalar(EA, rank, float(P), None, ALU.is_ge))
            st(dve.tensor_tensor(EA, EA, row(ADJ, TT), ALU.mult))
            st(dve.tensor_tensor(DS1, rank, row(E128, TT), ALU.add))
            st(dve.tensor_tensor(DS1, DS1, EA, ALU.add))
            for k, one in enumerate((O1, O2)):
                st(dve.tensor_tensor(EA, one, DS1, ALU.mult))
                st(dve.tensor_reduce(DEST[:, k, :], EA, AX.X, ALU.add))
            st(dve.tensor_copy(DESTI[:, :], DEST.rearrange("p a b -> p (a b)")))
            dve.sem_inc(routed, 1)

        def route_act(act, layer):
            act.wait_ge(cnt_ready, layer + 1)
            act.activation(EXR, EX, ACT.Exp).then_inc(lg_exp, 1)

        def route_pe(pe, layer):
            pe.wait_ge(cnt_ready, layer + 1)
            ones = ONES[:, 0:1].to_broadcast([P, P])
            for t in range(TT):
                for j in range(t + 1):
                    nc.tensor.matmul(AUX[:, 0, t * NE:(t + 1) * NE], tri if j == t else ones, CN[:, j, :],
                                     start=(j == 0), stop=(j == t))
            for j in range(TT):
                last = nc.tensor.matmul(AUX[:, 1, 0:NE], ones, CN[:, j, :], start=(j == 0), stop=(j == TT - 1))
            last.then_inc(rank_ps, 1)

        def build_pick(pool, g, o, first=False):
            st = o.step
            hold(pool, picked, g)
            if first:
                st(pool.tensor_copy(DD, DEST))
            for t in range(TT):
                st(pool.tensor_scalar(PICKB[:, t * P:(t + 1) * P], iota, DD[:, 1, t:t + 1], None, ALU.is_equal))
                st(pool.tensor_scalar(PICKA, iota, DD[:, 0, t:t + 1], None, ALU.is_equal))
                st(pool.tensor_tensor(PT[:, t, :], PICKA, PICKB[:, t * P:(t + 1) * P], ALU.add))
            st(pool.tensor_scalar(DD.rearrange("p a b -> p (a b)"), DD.rearrange("p a b -> p (a b)"),
                                  -float(P), None, ALU.add))
            pool.sem_inc(pick_ready, 1)
        PICK_STEPS = 13

        def blocks(eng, layer, n0, body, own_steps=None):
            base = 0 if layer == 0 else n0
            body(0, base, True)
            with eng.Fori(1, NE) as b:
                if own_steps:
                    own_steps[0].enter(b - 1, own_steps[1])
                body(b, b + base, False)
                if own_steps:
                    own_steps[0].leave(NE - 1)
            eng.wait_ge(over_set, layer + 1)
            n_over = eng.value_load(NBI[0:1, layer:layer + 1], min_val=0, max_val=MAX_OVER)
            with eng.Fori(0, MAX_OVER) as i:
                with eng.If(i < n_over):
                    if own_steps:
                        own_steps[0].enter(i, own_steps[1])
                    body(i + NE, i + NE + base, False)
                    if own_steps:
                        own_steps[0].leave(n_over)
            return n_over + NE, n_over + (NE + base)

        def combine_pool(pool, layer, N):
            hold(pool, y_store, N * 16 + 16 * RH)
            for t in range(TT):
                s = t % 2
                if t >= 2 or layer:
                    hold(pool, x_done, X_DONE[2 if layer == 0 else 5] - TT + t - 1)
                for k in range(2):
                    pool.indirect_dma_start(
                        out=sc(2048 * k + D * s, D), out_offset=None, in_=y_rows,
                        in_offset=bass.IndirectOffsetOnAxis(ap=DESTI[:, k * TT + t:k * TT + t + 1], axis=0),
                    ).then_inc(back_in[s], 16)

        def combine_act(act, layer):
            for t in range(TT):
                s = t % 2
                act.wait_ge(back_in[s], 32 * (2 * layer + t // 2 + 1))
                y1 = sc(D * s, D)
                act.activation(y1, y1, ACT.Copy, scale=WTS[:, 0, t:t + 1]).then_inc(back_act, 1)

        def combine_dve(dve, layer, o, gate_count):
            dve.wait_ge(gate_in, 16 * gate_count)
            for t in range(TT):
                s = t % 2
                y1, y2 = sc(D * s, D), sc(2048 + D * s, D)
                dve.wait_ge(back_in[s], 32 * (2 * layer + t // 2 + 1))
                dve.wait_ge(back_act, TT * layer + t + 1)
                o.step(dve.scalar_tensor_tensor(y2, y2, WTS[:, 1, t:t + 1], y1, ALU.mult, ALU.add))
                o.step(dve.tensor_tensor(y2, y2, GATE, ALU.mult))
                dve.tensor_tensor(X[:, t, :], X[:, t, :], y2, ALU.add).then_inc(x_done, 1)

        KT = sc(0, 4096).rearrange("p (h t) -> p h t", h=AHEADS)
        VV = sc(4096, 4096).rearrange("p (t n) -> p t n", t=TT)
        QT = sc(8192, 2048).rearrange("p (h t) -> p h t", h=4)
        KS, JK = sc(10240, 512), sc(10752, 128)
        ON = sc(10880, 256).rearrange("p (b n) -> p b n", b=2)
        SQ = RAW[:, 3, 0:1024].rearrange("p (b n) -> p b n", b=2)
        KN = RAW[:, 3, 1024:2048].rearrange("p (b n) -> p b n", b=2)
        EE = RAW[:, 3, :].rearrange("p (b t n) -> p b t n", b=2, t=2)
        GATE2, TMP2 = RAW[:, 3, 0:1024], RAW[:, 3, 1024:2048].rearrange("p (b n) -> p b n", b=2)

        def qk_norm_act(act, z, w, S, gain, dst, x_wait):
            def sq(t):
                act.wait_ge(pe_steps, fin(S, t))
                if x_wait is not None:
                    act.wait_ge(x_done, x_wait)
                act.activation(SQ[:, t % 2, :], ACC[:, t, :], ACT.Square).then_inc(a_sq, 1)
                act.wait_ge(a_ss, z * 4 + (t + 1))
                act.activation(st8b[:, 8 * (t % 2):8 * (t % 2) + 8], st8a[:, 8 * (t % 2):8 * (t % 2) + 8], ACT.Sqrt,
                               bias=eps, scale=1.0 / HD).then_inc(a_sd, 1)
            def out_T(t):
                act.wait_ge(a_T, z * 4 + (t + 1))
                act.activation(dst(t), AUX[:, t % 2, :].rearrange("p (h c) -> p h c", c=P), ACT.Copy,
                               scale=gain).then_inc(a_kv, 1)
            for t in range(TT):
                sq(t)
                if t:
                    out_T(t - 1)
            out_T(TT - 1)

        def qk_norm_dve(dve, z, o):
            for t in range(TT):
                a, b = st8a[:, 8 * (t % 2):8 * (t % 2) + 8], st8b[:, 8 * (t % 2):8 * (t % 2) + 8]
                dve.wait_ge(a_sq, z * 4 + (t + 1))
                dve.tensor_reduce(a, SQ[:, t % 2, :].rearrange("p (g d) -> p g d", d=HD), AX.X, ALU.add).then_inc(a_ss, 1)
                dve.wait_ge(a_sd, z * 4 + (t + 1))
                o.step(dve.reciprocal(b, b))
                if t >= 2:
                    dve.wait_ge(a_T, z * 4 + (t - 1))
                dve.tensor_tensor(KN[:, t % 2, :].rearrange("p (g d) -> p g d", d=HD),
                                  ACC[:, t, :].rearrange("p (g d) -> p g d", d=HD),
                                  col(b, HD), ALU.mult).then_inc(acc_free, 1)
        QK_STEPS = TT

        def qk_norm_pe(pe, z, w):
            for t in range(TT):
                pe.wait_ge(acc_free, w * 4 + (4 + t + 1))
                if t >= 2:
                    pe.wait_ge(a_kv, z * 4 + (t - 1))
                for j in range(4):
                    last = nc.tensor.transpose(AUX[:, t % 2, j * P:(j + 1) * P], KN[:, t % 2, j * P:(j + 1) * P], ident)
                last.then_inc(a_T, 1)

        UNITS = [(j, qb) for j in range(4) for qb in range(TT)]

        def mix_pos(g, i):
            arrived = {0: g + 3, 1: g * 2 + 4, 2: g + 4, 3: g * 2 + 5}[i]
            return HALF_SLOT[i], arrived

        qn8 = SM[:, 22:23]
        LAMV = sc(10240, 256)
        PV_BANK = {3: 1, 2: 2, 1: 0, 0: 1}
        ST_AT = [0, 512, 896, 1152]

        def head_y_hi(act, h, t):
            act.wait_ge(y_T, h * 4 + (t + 1))
            act.activation(bview(BH)[:, :, t * P:(t + 1) * P], AUX[:, t % 2, :].rearrange("p (k c) -> p k c", c=P),
                           ACT.Copy).then_inc(y_hi, 1)

        def head_y_lo(dve, h, t):
            dve.wait_ge(y_hi, h * 4 + (t + 1))
            dve.tensor_tensor(bview(BL)[:, :, t * P:(t + 1) * P], AUX[:, t % 2, :].rearrange("p (k c) -> p k c", c=P),
                              bview(BH)[:, :, t * P:(t + 1) * P].bitcast(F32), ALU.subtract).then_inc(y_lo, 1)

        def bview(b):
            return b[:, :].rearrange("p (k t) -> p k t", t=T)

        def residual_add(dve, o, steps, q, t, gate, tmp):
            cols = slice(q * 512, (q + 1) * 512)
            dve.wait_ge(pe_steps, steps)
            o.step(dve.tensor_tensor(tmp[:, t % 2, :], ACC[:, t, :], gate[:, cols], ALU.mult))
            dve.sem_inc(acc_free, 1)
            dve.tensor_tensor(X[:, t, cols], X[:, t, cols], tmp[:, t % 2, :], ALU.add).then_inc(x_done, 1)

        block = ctx.enter_context(nc.Block())

        @block.sync
        def _(sp):
            sp.dma_start(X[:, :, :], io["x"].rearrange("b (t p) d -> p (b t) d", p=P)).then_inc(x_in, 16)
            sp.wait_ge(started, 1)
            for m in range(PRE_CHUNKS):
                q = m // 2
                load_chunk(sp, m % RING, k_rows(io["ada_w"][0:1, :, q * 512:(q + 1) * 512], 4, m % 2), 4, m + 1)
            with sp.Fori(0, RH) as h:
                for i, what in enumerate(HEAD_ORDER):
                    C, slot, _ = head_pos(h, i)
                    if what == "a":
                        a = sum(x == "a" for x in HEAD_ORDER[:i])
                        load_chunk(sp, slot, k_rows(head_half(h, a // 2)[0], 4, a % 2), 4, C + 1)
                    elif what < 2:
                        load_chunk(sp, slot, k_rows(io["ret_w_in"][0:1, :, ds(h * RK + what * 1024, RK)], 8, 0), 8, C + 1)
                    elif what < 6:
                        col0 = h * RV + (2048 if what < 4 else 4096)
                        load_chunk(sp, slot, k_rows(io["ret_w_in"][0:1, :, ds(col0, RV)], 4, what % 2), 4, C + 1)
                    else:
                        n = (what - 6) * 512
                        load_chunk(sp, slot, k_rows(io["ret_w_out"][0:1, ds(h * RV, RV), n:n + 512], 4, 0), 4, C + 1)
            def experts(layer, n0):
                c0 = moe_c(layer, n0)
                base = 0 if layer == 0 else n0
                expert_load(sp, layer, c0, 0, 0, True)
                with sp.Fori(1, NE) as e:
                    expert_load(sp, layer, c0, e, e, False)
                sp.wait_ge(over_set, layer + 1)
                n_over = sp.value_load(NBI[0:1, layer:layer + 1], min_val=0, max_val=MAX_OVER)
                with sp.Fori(0, MAX_OVER) as i:
                    with sp.If(i < n_over):
                        expert = sp.value_load(OEI[0:1, ds(i, 1)], min_val=0, max_val=NE - 1)
                        expert_load(sp, layer, c0, i + NE, expert, False)
                return n_over + (NE + base)
            n0 = experts(0, None)
            c0 = moe_c(1, n0) - MIX_CHUNKS
            kv = io["kv_w"].rearrange("(o k) n -> o k n", o=1)
            for m in range(8):
                u, q = m // 2, m % 2
                load_chunk(sp, KV_SLOT[m], k_rows(kv[:, :, u * 512:(u + 1) * 512], 4, q), 4, c0 + (m + 2 if m >= 3 else 4))
            with sp.Fori(0, 2) as g:
                for i in range(4):
                    if i < 2:
                        src = k_rows(io["diff_w_q"][0:1, :, ds(g * 512, 512)], 4, i)
                    else:
                        src = k_rows(io["diff_w_out"][0:1, ds(g * 512, 512), (i - 2) * 512:(i - 1) * 512], 4, 0)
                    load_chunk(sp, mix_pos(g, i)[0], src, 4, g * 4 + c0 + (8 + i + (3 if i % 2 else 2)))
            sp.wait_ge(s_olo, 2 * len(UNITS))
            sp.wait_ge(x_done, X_DONE[4])
            experts(1, n0)

        @block.gpsimd
        def _(pool):
            o = Own(pool, "pool")
            pool.dma_start(cT, io["c"].rearrange("b (k p) -> p (b k)", p=P), allow_slow_non_contiguous=True).then_inc(c_in, 16)
            pool.dma_start(TAB[:, :], io["table"]).then_inc(table_in, 16)
            for q in range(4):
                ada_store(pool, q, io["ada_b"][0:1, q * 512:(q + 1) * 512], slice(q, q + 1))
            hold(pool, row_out, 64)
            norm_pool(pool, 0)
            pool.dma_start(ROPE[:, 0, :, :], io["rope"][0:1, :, :].rearrange("o (t p) d -> p (o t) d", p=P)).then_inc(rope_in, 16)
            pool.dma_start(ROPE[:, 1, :, :], io["rope"][1:2, :, :].rearrange("o (t p) d -> p (o t) d", p=P)).then_inc(rope_in, 16)
            for i, name in enumerate(("q_norm", "k_norm")):
                v = (io[name] if name == "q_norm" else io[name].rearrange("(o d) -> o d", o=1)).rearrange("o d -> d o")
                for z in range(2):
                    pool.dma_start(SM[z * HD:(z + 1) * HD, 17 + i:18 + i], v, allow_slow_non_contiguous=True).then_inc(cols_in, 16)
            pool.dma_start(subln, io["diff_subln"].rearrange("o d -> d o"), allow_slow_non_contiguous=True).then_inc(cols_in, 16)
            pool.memset(PICKA, 0.0).then_inc(zero_set, 1)
            hold(pool, zero_set, 1)
            with pool.Fori(0, RH) as h:
                pool.dma_start(y_rows[ds(h * 2 * P + NE * P, 2 * P), :].rearrange("(p r) (k c) -> p (r k) c", p=P, c=P),
                               PICKA.rearrange("p (o c) -> p o c", o=1).broadcast_to([P, 16, P])).then_inc(y_store, 16)
                hold(pool, acc_free, h * 20 + 4)
                pool.dma_start(DEC, io["decay"][ds(h, 1), :, :].rearrange("o p n -> p (o n)")).then_inc(head_in, 16)
                pool.dma_start(GN, io["ret_gn"][0:1, ds(h * RV, RV)].broadcast_to([P, RV])).then_inc(head_in, 16)
                for j in range(6):
                    _, bias, flat = head_half(h, j)
                    ada_store(pool, h * 6 + (4 + j), bias, flat)
                    if j == 1:
                        with pool.If(h < 1):
                            hold(pool, row_out, 96)
                            pool.dma_start(GATE, rows2[2:3, :].broadcast_to([P, D])).then_inc(gate_in, 16)
            def moe_prelude(n, gate_row):
                layer = int(n == 4)
                norm_pool(pool, n)
                pool.dma_start(WR[:, :, 0:NG], k_rows(io["moe_w_group"][layer:layer + 1], 8, 0)).then_inc(lg_in, 16)
                pool.dma_start(WR[:, :, NG:20], k_rows(io["moe_w_expert"][layer:layer + 1], 8, 0)).then_inc(lg_in, 16)
                pool.dma_start(BR[:, 0:NG], io["moe_b_group"][layer:layer + 1, :].broadcast_to([P, NG])).then_inc(lg_in, 16)
                pool.dma_start(BR[:, NG:20], io["moe_b_expert"][layer:layer + 1, :].broadcast_to([P, NE])).then_inc(lg_in, 16)
                hold(pool, x_done, X_DONE[n])
                pool.dma_start(GATE, rows2[gate_row:gate_row + 1, :].broadcast_to([P, D])).then_inc(gate_in, 16)

            def moe(layer, n0):
                base = 0 if layer == 0 else n0
                hold(pool, routed, layer + 1)
                build_pick(pool, base + layer, o, first=True)

                def body(b, B, first):
                    build_pick(pool, B + (layer + 1), o)
                    if not first:
                        y_out_pool(pool, layer, b - 1, B - 1)
                n, N = blocks(pool, layer, n0, body, (o, PICK_STEPS))
                y_out_pool(pool, layer, n - 1, N - 1)
                combine_pool(pool, layer, N)
                return N

            hold(pool, row_out, 16 * HALVES)
            hold(pool, y_store, 16 * RH)
            hold(pool, y_lo, 16)
            moe_prelude(1, 5)
            n0 = moe(0, None)
            hold(pool, x_done, X_DONE[2])
            norm_pool(pool, 2)
            pool.dma_start(LAMV, io["diff_lam"].rearrange("o a d -> o (a d)").broadcast_to([P, 4 * HD])).then_inc(lam_in, 16)
            hold(pool, acc_free, 84 + 16)
            norm_pool(pool, 3)
            with pool.Fori(0, 2) as g:
                for j in range(4):
                    hold(pool, a_kv, g * 4 + 12)
                    if j:
                        hold(pool, s_ps, g * 16 + 4 * j)
                    pool.tensor_copy(KS, KT[:, ds(g * 4 + j, 1), :].rearrange("p o t -> p (o t)")).then_inc(ks_in, 1)
                hold(pool, s_olo, g * 16 + 16)
                pool.dma_start(GATE2, rows2[10:11, :].broadcast_to([P, D])).then_inc(gate_in, 16)
            moe_prelude(4, 13)
            moe(1, n0)
            for t in range(TT):
                hold(pool, x_done, X_DONE[5] - TT + t + 1)
                pool.dma_start(out[0, t * P:(t + 1) * P, :], X[:, t, :]).then_inc(out_done, 16)
            hold(pool, out_done, 16 * TT)

        @block.scalar
        def _(act):
            o = Own(act, "act")
            act.wait_ge(started, 1)
            act.wait_ge(c_in, 16)
            act.activation(cT, cT, ACT.Silu).then_inc(cact_done, 1)
            norm_act_stats(act, 0, o)
            norm_act_hi(act, 0)

            with act.Fori(0, RH) as h:
                def hi(i):
                    _, slot, arrived = head_pos(h, AT_SPLIT[i])
                    split_hi(act, slot, i % RING, arrived, free_steps(h * HEAD_SPLIT + i))
                o.enter(h, TT)
                for i in range(4):
                    hi(i)
                for t in range(TT):
                    act.wait_ge(qk_T, h * 4 + (t + 1))
                    act.activation(qkT[:, :, t * P:(t + 1) * P], AUX[:, t % 2, :].rearrange("p (j c) -> p j c", c=P),
                                   ACT.Copy).then_inc(qk_out, 1)
                hi(4)
                for t in range(TT):
                    act.wait_ge(pe_steps, fin(h * HEAD_SPLIT + 3, t))
                    act.activation(V1[:, t, :], ACC[:, t, :], ACT.Copy).then_inc(acc_free, 1)
                hi(5)
                for n, t in enumerate(reversed(range(TT))):
                    act.wait_ge(pv_ps, h * 4 + (n + 1))
                    o.step(act.activation(SG[:, 0, :], AUX[:, PV_BANK[t], :], ACT.Square, accum_out=so[:, n:n + 1]))
                    act.activation(sd_o[:, n:n + 1], so[:, n:n + 1], ACT.Sqrt, bias=eps, scale=1.0 / RV).then_inc(o_sd, 1)
                hi(6)
                hi(7)
                for t in range(TT):
                    act.wait_ge(pe_steps, fin(h * HEAD_SPLIT + 5, t))
                    if t >= 2:
                        act.wait_ge(y_done, h * 4 + (t - 1))
                    act.activation(SG[:, t % 2, :], ACC[:, t, :], ACT.Silu).then_inc(silu_done, 1)
                    if t:
                        head_y_hi(act, h, t - 1)
                head_y_hi(act, h, TT - 1)
                o.leave(RH)
            def moe(layer, n0):
                moe_norm_act(act, 1 if layer == 0 else 4, o)
                route_act(act, layer)
                base = 0 if layer == 0 else n0
                tokens_hi(act, base + layer)
                s0 = moe_s(layer, n0)
                n, N = blocks(act, layer, n0, lambda b, B, first: expert_act(act, layer, n0, s0, b, B, first))
                y_out_act(act, n * MOE_CHUNKS + s0 - 1, N - 1)
                combine_act(act, layer)
                return N
            n0 = moe(0, None)
            act.wait_ge(lam_sum, 1)
            act.activation(lam_s[:, 2:4], lam_s[:, 0:2], ACT.Exp).then_inc(lam_exp, 1)
            norm_act_stats(act, 2, o)
            norm_act_hi(act, 2)
            s0 = moe_s(1, n0) - MIX_CHUNKS
            a0 = [n0 * 3 + (C_MOE0 // RING)] * 3
            for u in range(4):
                for q in range(2):
                    m = 2 * u + q
                    split_hi(act, KV_SLOT[m], m % RING, a0[0] + (m // 3 + 1), free_steps(s0 + m))
                if u < 2:
                    qk_norm_act(act, u, u, s0 + 2 * u + 1, kn_g, lambda t, u=u: KT[:, 4 * u:4 * u + 4, t * P:(t + 1) * P], None)
                else:
                    for t in range(TT):
                        act.wait_ge(pe_steps, fin(s0 + 2 * u + 1, t))
                        act.activation(VV[:, t, (u - 2) * 512:(u - 1) * 512], ACC[:, t, :], ACT.Copy).then_inc(acc_free, 1)
            norm_act_hi(act, 3)
            with act.Fori(0, 2) as g:
                def hi(i):
                    slot, arrived = mix_pos(g, i)
                    split_hi(act, slot, i % RING, arrived + a0[0], free_steps(g * 4 + s0 + (8 + i)))
                o.enter(g, len(UNITS))
                hi(0)
                hi(1)
                qk_norm_act(act, g + 2, None, g * 4 + s0 + 9, qn8, lambda t: QT[:, :, t * P:(t + 1) * P], g * 8 + 36)
                hi(2)
                hi(3)

                def exps(u):
                    p, vis = u % 2, (UNITS[u][1] + 1) * P
                    act.wait_ge(s_max, g * 16 + (u + 1))
                    for t in range(2):
                        if t == 0 and u >= 2:
                            act.wait_ge(s_o, g * 16 + (u - 1))
                        act.activation(EE[:, p, t, 0:vis], ACC[:, 2 * p + t, 0:vis], ACT.Exp, bias=att[:, 2 * p + t:2 * p + t + 1],
                                       scale=1.0, accum_out=att[:, 4 + 2 * p + t:5 + 2 * p + t]).then_inc(s_exp, 1)

                def copy_T(u):
                    p, vis = u % 2, (UNITS[u][1] + 1) * P
                    act.wait_ge(s_aT, g * 16 + (u + 1))
                    act.activation(EE[:, p, 1, 0:vis], AUX[:, p, 0:vis], ACT.Copy).then_inc(s_at, 1)

                def o_stats(u):
                    p = u % 2
                    act.wait_ge(s_o, g * 16 + (u + 1))
                    o.step(act.activation(JK, AUX[:, 2 + p, 0:P], ACT.Square, accum_out=so[:, p:p + 1]))
                    act.activation(sd_o[:, p:p + 1], so[:, p:p + 1], ACT.Sqrt, bias=eps, scale=1.0 / P).then_inc(s_so, 1)

                def o_hi(u):
                    p, (j, qb) = u % 2, UNITS[u]
                    act.wait_ge(s_oT, g * 16 + (u + 1))
                    act.activation(BH[:, j * T + qb * P:j * T + (qb + 1) * P], AUX[:, 2 + p, P:2 * P], ACT.Copy,
                                   scale=subln).then_inc(s_ohi, 1)
                for u in range(len(UNITS) + 2):
                    if u < len(UNITS):
                        exps(u)
                    if 1 <= u <= len(UNITS):
                        copy_T(u - 1)
                        o_stats(u - 1)
                    if u >= 2:
                        o_hi(u - 2)
                o.leave(2)
            moe(1, n0)

        @block.tensor
        def _(pe):
            pe.wait_ge(started, 1)
            pe.wait_ge(table_in, 16)
            for q in range(4):
                ada_sum(pe, q)
            for t in range(TT):
                norm_pe(pe, 0, t)
            pe.wait_ge(n_lo, TT)
            with pe.Fori(0, RH) as h:
                S = h * HEAD_SPLIT

                def C(i):
                    return head_pos(h, AT_SPLIT[i])[0]

                def q_of(j):
                    return h * 6 + (4 + j)

                def after_qk(q, t):
                    if q == 1 and t == 3:
                        ada_sum(pe, q_of(0))

                def after_v(q, t):
                    if q == 0:
                        pe.wait_ge(rot_done, h * 4 + (t + 1))
                        if t >= 2:
                            pe.wait_ge(qk_out, h * 4 + (t - 1))
                        for j in range(4):
                            last = nc.tensor.transpose(AUX[:, t % 2, j * P:(j + 1) * P], QKR[:, t % 2, j * P:(j + 1) * P], ident)
                        last.then_inc(qk_T, 1)
                        if t == 3:
                            ada_sum(pe, q_of(1))
                    elif t == 3:
                        ada_sum(pe, q_of(2))

                def y_T_(t):
                    pe.wait_ge(y_done, h * 4 + (t + 1))
                    if t >= 2:
                        pe.wait_ge(y_lo, h * 4 + (t - 1))
                    for k in range(4):
                        last = nc.tensor.transpose(AUX[:, t % 2, k * P:(k + 1) * P], V1[:, t, k * P:(k + 1) * P], ident)
                    last.then_inc(y_T, 1)

                def after_g(q, t):
                    if q == 0 and t == 3:
                        ada_sum(pe, q_of(3))
                    if q == 1 and t == 0:
                        ada_sum(pe, q_of(4))
                    if q == 1 and t:
                        y_T_(t - 1)

                project(pe, (S, 0), (C(0), C(1)), h * 5, hT(AH), hT(AL), after_qk, halves=2)
                project(pe, (S, 2), (C(2), C(3)), h * 5 + 1, hT(AH), hT(AL), after_v)
                pe.wait_ge(qk_out, h * 4 + 4)
                for m in range(TT):
                    if m == 3:
                        pe.wait_ge(st_done, h * 4 + 1)
                    n = T - m * P
                    for k in range(2):
                        last = nc.tensor.matmul(AUX[:, m % 3, 0:n], qkT[:, 2 + k, m * P:(m + 1) * P], qkT[:, k, m * P:T],
                                                start=(k == 0), stop=(k == 1))
                    last.then_inc(st_ps, 1)
                pe.wait_ge(st_done, h * 4 + 4)
                pe.wait_ge(acc_free, h * 20 + 12)
                for t in reversed(range(TT)):
                    if t == 0:
                        pe.wait_ge(o_norm, h * 4 + 1)
                    for m in range(t + 1):
                        at_ = ST_AT[m] + (t - m) * P
                        last = nc.tensor.matmul(AUX[:, PV_BANK[t], :], ST[:, at_:at_ + P], V1[:, m, :],
                                                start=(m == 0), stop=(m == t))
                    last.then_inc(pv_ps, 1)
                project(pe, (S, 4), (C(4), C(5)), h * 5 + 2, hT(AH), hT(AL), after_g)
                y_T_(3)
                for q in range(2):
                    out_project(pe, 6 + q, C(6 + q), h * 5 + (3 + q), q,
                                (lambda t: pe.wait_ge(y_lo, h * 4 + (t + 1))) if q == 0 else None)
                    if q == 0:
                        ada_sum(pe, q_of(5))
            def moe(layer, n0):
                moe_norm_pe(pe, 1 if layer == 0 else 4)
                route_pe(pe, layer)
                base = 0 if layer == 0 else n0
                pe.wait_ge(over_set, layer + 1)
                pe.wait_ge(routed, layer + 1)
                pe.wait_ge(n_lo, TT * (2 if layer == 0 else 5))
                pick_tokens(pe, base + layer, 0)
                pick_tokens(pe, base + layer, 1)
                c0, s0 = moe_c(layer, n0), moe_s(layer, n0)
                return blocks(pe, layer, n0, lambda b, B, first: expert_pe(pe, layer, c0, s0, b, B))[1]
            n0 = moe(0, None)
            for t in range(TT):
                norm_pe(pe, 2, t)
            pe.wait_ge(n_lo, TT * 3)
            c0, s0 = moe_c(1, n0) - MIX_CHUNKS, moe_s(1, n0) - MIX_CHUNKS
            for u in range(4):
                project(pe, (s0, 2 * u), (c0 + 2 * u, c0 + 2 * u + 1), 20 + u, hT(AH), hT(AL))
                if u < 2:
                    qk_norm_pe(pe, u, 20 + u)
            for t in range(TT):
                norm_pe(pe, 3, t)
            pe.wait_ge(n_lo, TT * 4)
            with pe.Fori(0, 2) as g:
                w = g * 3 + 24
                U0 = g * 16
                project(pe, (s0, 0), (g * 4 + c0 + 8, g * 4 + c0 + 9), w, hT(AH), hT(AL))
                qk_norm_pe(pe, g + 2, w)
                pe.wait_ge(a_kv, g * 4 + 12)
                pe.wait_ge(acc_free, w * 4 + 8)

                def scores(u):
                    p, (j, qb) = u % 2, UNITS[u]
                    vis = (qb + 1) * P
                    if qb == 0:
                        pe.wait_ge(ks_in, g * 4 + (j + 1))
                    if u >= 2:
                        pe.wait_ge(s_exp, g * 32 + 2 * (u - 1))
                    for t in range(2):
                        rows = slice(t * HD, (t + 1) * HD)
                        last = nc.tensor.matmul(ACC[:, 2 * p + t, 0:vis], QT[rows, j, qb * P:(qb + 1) * P], KS[rows, 0:vis],
                                                start=True, stop=True)
                    last.then_inc(s_ps, 1)

                def a_T_(u):
                    p, (j, qb) = u % 2, UNITS[u]
                    pe.wait_ge(s_a, U0 + (u + 1))
                    if u >= 2:
                        pe.wait_ge(s_at, U0 + (u - 1))
                    for k in range(qb + 1):
                        last = nc.tensor.transpose(AUX[:, p, k * P:(k + 1) * P], EE[:, p, 0, k * P:(k + 1) * P], ident)
                    last.then_inc(s_aT, 1)

                def pv(u):
                    p, (j, qb) = u % 2, UNITS[u]
                    pe.wait_ge(s_at, U0 + (u + 1))
                    if u >= 2:
                        pe.wait_ge(s_olo, U0 + (u - 1))
                    for k in range(qb + 1):
                        v = VV[:, k, ds(g * 512 + j * P, P)]
                        last = nc.tensor.matmul(AUX[:, 2 + p, 0:P], EE[:, p, 1, k * P:(k + 1) * P], v,
                                                start=(k == 0), stop=(k == qb))
                    last.then_inc(s_o, 1)

                def o_T(u):
                    p = u % 2
                    pe.wait_ge(s_on, U0 + (u + 1))
                    nc.tensor.transpose(AUX[:, 2 + p, P:2 * P], ON[:, p, :], ident).then_inc(s_oT, 1)
                scores(0)
                for u in range(len(UNITS) + 1):
                    if u + 1 < len(UNITS):
                        scores(u + 1)
                    if u < len(UNITS):
                        a_T_(u)
                        pv(u)
                    if u >= 1:
                        o_T(u - 1)
                pe.wait_ge(s_olo, U0 + 16)
                for q in range(2):
                    out_project(pe, 2 + q, g * 4 + c0 + (10 + q), w + (1 + q), q, None)
            moe(1, n0)

        @block.vector
        def _(dve):
            o = Own(dve, "dve")
            o.step(dve.memset(ONES[:, :], 1.0))
            o.step(dve.memset(eps, EPS))
            dve.memset(credit, 0.0).then_inc(raw_used, RING)
            dve.sem_inc(pe_steps, 4 * RING)
            dve.sem_inc(acc_free, TT)
            dve.sem_inc(started, 3)
            dve.wait_ge(cact_done, 1)
            for q in range(4):
                ada_acc(dve, o, q, [(2 * q) % RING, (2 * q + 1) % RING], [(2 * q) // RING + 1, (2 * q + 1) // RING + 1])
                ada_row(dve, q)
            norm_dve(dve, 0, o)
            HEAD_STEPS = 6 * 8 + 8 + 4 + 8
            with dve.Fori(0, RH) as h:
                o.enter(h, HEAD_STEPS)

                def lo(i):
                    _, slot, arrived = head_pos(h, AT_SPLIT[i])
                    split_lo(dve, slot, i % RING, arrived, free_steps(h * HEAD_SPLIT + i), h * HEAD_SPLIT + (i + 1))

                def ada(j):
                    q = h * 6 + (4 + j)
                    pos = [head_pos(h, i) for i in AT_ADA[j]]
                    ada_acc(dve, o, q, [x[1] for x in pos], [x[2] for x in pos])

                def arow(j):
                    ada_row(dve, h * 6 + (4 + j))
                lo(0)
                ada(0)
                lo(1)
                for t in range(TT):
                    dve.wait_ge(pe_steps, fin(h * HEAD_SPLIT + 1, t))
                    if t == 0:
                        dve.wait_ge(rope_in, 32)
                    x4 = ACC[:, t, :].rearrange("p (z d) -> p z d", d=P)
                    cs = row(ROPE[:, 0, t, :], 4)
                    sn = row(ROPE[:, 1, t, :], 4)
                    a4, b4 = (ROT[:, i, :].rearrange("p (z d) -> p z d", d=P) for i in range(2))
                    dve.tensor_tensor(a4, x4, cs, ALU.mult)
                    o.step(dve.tensor_tensor(b4, x4, sn, ALU.mult))
                    dve.sem_inc(acc_free, 1)
                    if t >= 2:
                        dve.wait_ge(qk_T, h * 4 + (t - 1))
                    r = QKR[:, t % 2, :].rearrange("p (z s d) -> p z s d", s=2, d=P)
                    a2, b2 = (ROT[:, i, :].rearrange("p (z s d) -> p z s d", s=2, d=P) for i in range(2))
                    dve.tensor_tensor(r[:, :, 0, :], a2[:, :, 0, :], b2[:, :, 1, :], ALU.subtract)
                    o.step(dve.tensor_tensor(r[:, :, 1, :], a2[:, :, 1, :], b2[:, :, 0, :], ALU.add))
                    dve.sem_inc(rot_done, 1)
                    if t == 0:
                        arow(0)
                        ada(1)
                        lo(2)
                arow(1)
                ada(2)
                lo(3)
                arow(2)
                ada(3)
                lo(4)
                dve.wait_ge(head_in, h * 32 + 32)
                for m in range(TT):
                    dve.wait_ge(st_ps, h * 4 + (m + 1))
                    n = T - m * P
                    dve.tensor_tensor(ST[:, ST_AT[m]:ST_AT[m] + n], AUX[:, m % 3, 0:n], DEC[:, 0:n], ALU.mult).then_inc(st_done, 1)
                for n, t in enumerate(reversed(range(TT))):
                    dve.wait_ge(o_sd, h * 4 + (n + 1))
                    o.step(dve.reciprocal(sd_o[:, n:n + 1], sd_o[:, n:n + 1]))
                    dve.scalar_tensor_tensor(V1[:, t, :], AUX[:, PV_BANK[t], :], sd_o[:, n:n + 1], GN, ALU.mult,
                                             ALU.mult).then_inc(o_norm, 1)
                arow(3)
                ada(4)
                lo(5)
                arow(4)
                ada(5)
                lo(6)
                lo(7)
                dve.wait_ge(o_norm, h * 4 + 4)
                for t in range(TT):
                    dve.wait_ge(silu_done, h * 4 + (t + 1))
                    dve.tensor_tensor(V1[:, t, :], V1[:, t, :], SG[:, t % 2, :], ALU.mult).then_inc(y_done, 1)
                    dve.sem_inc(acc_free, 1)
                    if t:
                        head_y_lo(dve, h, t - 1)
                head_y_lo(dve, h, TT - 1)
                dve.wait_ge(gate_in, 16)
                for q in range(2):
                    if q == 1:
                        arow(5)
                    for t in range(TT):
                        residual_add(dve, o, fin(h * HEAD_SPLIT + (6 + q), t), q, t, GATE, TMP)
                o.leave(RH)
            def moe(layer, n0, gate_count):
                moe_norm_dve(dve, 1 if layer == 0 else 4, o)
                route_dve(dve, layer, o)
                base = 0 if layer == 0 else n0
                tokens_lo(dve, base + layer)
                c0, s0 = moe_c(layer, n0), moe_s(layer, n0)
                n, N = blocks(dve, layer, n0, lambda b, B, first: expert_dve(dve, layer, n0, c0, s0, b, B, first))
                y_out_dve(dve, n * MOE_CHUNKS + s0 - 1, N - 1)
                combine_dve(dve, layer, o, gate_count)
                return N
            n0 = moe(0, None, 2)
            dve.wait_ge(lam_in, 16)
            for i in range(2):
                o.step(dve.tensor_tensor(JK[:, 0:HD], LAMV[:, 2 * i * HD:(2 * i + 1) * HD], LAMV[:, (2 * i + 1) * HD:(2 * i + 2) * HD],
                                         ALU.mult))
                o.step(dve.tensor_reduce(lam_s[:, i:i + 1], JK[:, 0:HD], AX.X, ALU.add))
            dve.wait_ge(cols_in, 16 * 5)
            o.step(dve.tensor_scalar(qn8, qn, HD ** -0.5, None, ALU.mult))
            dve.sem_inc(lam_sum, 1)
            dve.wait_ge(lam_exp, 1)
            o.step(dve.tensor_tensor(nlam, lam_s[:, 3:4], lam_s[:, 2:3], ALU.subtract))
            o.step(dve.tensor_scalar(nlam, nlam, -LAMBDA_INIT, None, ALU.add))
            norm_dve(dve, 2, o)
            s0 = moe_s(1, n0) - MIX_CHUNKS
            a0 = n0 * 3 + (C_MOE0 // RING)
            for u in range(4):
                for q in range(2):
                    m = 2 * u + q
                    split_lo(dve, KV_SLOT[m], m % RING, a0 + (m // 3 + 1), free_steps(s0 + m), s0 + m + 1)
                if u < 2:
                    qk_norm_dve(dve, u, o)
            norm_dve(dve, 3, o)
            with dve.Fori(0, 2) as g:
                def lo(i):
                    slot, arrived = mix_pos(g, i)
                    S = g * 4 + s0 + (8 + i)
                    split_lo(dve, slot, i % RING, arrived + a0, free_steps(S), S + 1)
                o.enter(g, QK_STEPS + 5 * len(UNITS) + 8)
                lo(0)
                lo(1)
                qk_norm_dve(dve, g + 2, o)
                lo(2)
                lo(3)

                def maxima(u):
                    p, vis = u % 2, (UNITS[u][1] + 1) * P
                    dve.wait_ge(s_ps, g * 16 + (u + 1))
                    o.step(dve.memset(ACC[0:CHUNK, 2 * p:2 * p + 2, vis - CHUNK:vis], -BIG))
                    dve.tensor_reduce(att[:, 2 * p:2 * p + 2], ACC[:, 2 * p:2 * p + 2, 0:vis], AX.X, ALU.max,
                                      negate=True).then_inc(s_max, 1)

                def mix(u):
                    p, vis = u % 2, (UNITS[u][1] + 1) * P
                    r = att[:, 8 + 2 * p:10 + 2 * p]
                    dve.wait_ge(s_exp, g * 32 + (2 * u + 2))
                    o.step(dve.reciprocal(r, att[:, 4 + 2 * p:6 + 2 * p]))
                    o.step(dve.tensor_tensor(r[:, 1:2], r[:, 1:2], nlam, ALU.mult))
                    o.step(dve.tensor_scalar(EE[:, p, 1, 0:vis], EE[:, p, 1, 0:vis], r[:, 1:2], None, ALU.mult))
                    dve.scalar_tensor_tensor(EE[:, p, 0, 0:vis], EE[:, p, 0, 0:vis], r[:, 0:1], EE[:, p, 1, 0:vis],
                                             ALU.mult, ALU.add).then_inc(s_a, 1)

                def o_scale(u):
                    p = u % 2
                    dve.wait_ge(s_so, g * 16 + (u + 1))
                    if u >= 2:
                        dve.wait_ge(s_oT, g * 16 + (u - 1))
                    o.step(dve.reciprocal(sd_o[:, p:p + 1], sd_o[:, p:p + 1]))
                    dve.tensor_scalar(ON[:, p, :], AUX[:, 2 + p, 0:P], sd_o[:, p:p + 1], 1.0 - LAMBDA_INIT,
                                      ALU.mult, ALU.mult).then_inc(s_on, 1)

                def o_lo(u):
                    p, (j, qb) = u % 2, UNITS[u]
                    at_ = slice(j * T + qb * P, j * T + (qb + 1) * P)
                    dve.wait_ge(s_ohi, g * 16 + (u + 1))
                    dve.scalar_tensor_tensor(BL[:, at_], AUX[:, 2 + p, P:2 * P], subln, BH[:, at_].bitcast(F32),
                                             ALU.mult, ALU.subtract).then_inc(s_olo, 1)
                maxima(0)
                for u in range(len(UNITS) + 2):
                    if u < len(UNITS):
                        mix(u)
                    if u + 1 < len(UNITS):
                        maxima(u + 1)
                    if 1 <= u <= len(UNITS):
                        o_scale(u - 1)
                    if u >= 2:
                        o_lo(u - 2)
                dve.wait_ge(gate_in, g * 16 + 48)
                for q in range(2):
                    for t in range(TT):
                        residual_add(dve, o, fin(g * 4 + s0 + (10 + q), t), q, t, GATE2, TMP2)
                o.leave(2)
            moe(1, n0, 5)


_INS = ["x", "c", "ada_w", "ada_b", "norm_mix", "norm_ffn", "ret_w_in", "ret_gn", "ret_w_out", "kv_ada_w", "kv_ada_b",
        "kv_norm", "kv_w", "k_norm", "diff_w_q", "q_norm", "diff_lam", "diff_subln", "diff_w_out", "moe_w_group",
        "moe_b_group", "moe_w_expert", "moe_b_expert", "moe_w1", "moe_w3", "moe_w2"]


def kernel(**inputs):
    import concourse.bacc as bacc
    from concourse.bass_utils import run_bass_kernel_spmd

    nc = bacc.Bacc("TRN2", target_bir_lowering=False, num_devices=1)
    arrays, io = {}, {}
    for name, a in [(n, inputs[n]) for n in _INS] + list(shape_constants().items()):
        a = np.ascontiguousarray(a)
        arrays[f"in_{name}"] = a
        io[name] = nc.dram_tensor(f"in_{name}", a.shape, mybir.dt.from_np(a.dtype), kind="ExternalInput").ap()
    out = nc.dram_tensor("out_x", (1, T, D), F32, kind="ExternalOutput").ap()
    build_trunk(nc, io, out)
    r = run_bass_kernel_spmd(nc, [arrays], core_ids=[0])
    return r.results[0]["out_x"]
```

```python
import math
from contextlib import ExitStack

import numpy as np

import concourse.bass as bass
from concourse import mybir
from concourse.alu_op_type import AluOpType as ALU

F32 = mybir.dt.float32
F32R = mybir.dt.float32r
I32 = mybir.dt.int32
ACT = mybir.ActivationFunctionType
AX = mybir.AxisListType
ds = bass.ds

P = 128
T = 512
D = 1024
TT = T // P
KD = D // P
EPS = 1e-6
RH, RK, RV = 4, 256, 512
AHEADS, HD = 8, 64
LAMBDA_INIT = 0.8 - 0.6 * math.exp(-0.3)
CHUNK = 64
NG, EPG = 4, 4
NE = NG * EPG
MAX_OVER = (2 * T) // (P + 1)
Y_BLOCKS = NE + 2 * RH
assert Y_BLOCKS >= NE + MAX_OVER
BIG = 1e30

RING = 4
PRE_CHUNKS = 8
HEAD_CHUNKS, HEAD_SPLIT = 20, 8
MOE_CHUNKS = 12
MIX_CHUNKS = 16
HALVES = 28
HEAD_ORDER = [0, "a", "a", 1, "a", "a", 2, "a", "a", 3, "a", "a", 4, "a", "a", 5, "a", "a", 6, 7]
KV_SLOT = [0, 1, 2, 0, 1, 2, 0, 1, 0, 1]
HALF_SLOT = [0, 1, 2, 0]
SLOT_BACK = [1, 2, 4, 3]


def shape_constants():
    table = np.zeros((P, 3 * P), np.float32)
    table[:, 0:P] = np.eye(P)
    table[:, P:2 * P] = np.triu(np.ones((P, P)), 1)
    table[:, 2 * P:3 * P] = np.arange(P)[None, :]
    half = RK // 2
    inv = (1.0 / (np.float32(10000.0) ** (np.arange(half, dtype=np.float32) / np.float32(half)))).astype(np.float32)
    ang = (np.arange(T, dtype=np.float32)[:, None] * inv[None, :]).astype(np.float32)
    rope = np.stack([np.cos(ang), np.sin(ang)]).astype(np.float32)
    decay = np.zeros((RH, P, T), np.float64)
    log_gamma = np.log1p(-np.exp2(-5.0 - np.arange(RH)))
    rel = np.arange(T)[None, :] - np.arange(P)[:, None]
    for h in range(RH):
        decay[h] = np.where(rel >= 0, np.exp(rel * log_gamma[h]), 0.0) * RK ** -0.5
    return {"table": table, "rope": rope, "decay": decay.astype(np.float32)}


def build_trunk(nc, io, out):
    ctx = ExitStack()

    def sb(name, shape, dt=F32):
        return ctx.enter_context(nc.sbuf_tensor(name, shape, dt))

    def sem(name):
        return ctx.enter_context(nc.semaphore(name))

    with ctx:
        AH = sb("act_hi", [P, KD, T], F32R)
        AL = sb("act_lo", [P, KD, T], F32R)
        BH = sb("act2_hi", [P, 2048], F32R)
        BL = sb("act2_lo", [P, 2048], F32R)
        WH = sb("w_hi", [P, RING, 2048], F32R)
        WL = sb("w_lo", [P, RING, 2048], F32R)
        PT = sb("pick", [P, TT, P], F32R)
        RAW = sb("w_raw", [P, RING, 2048])
        X = sb("x_res", [P, TT, D])
        TAB = sb("table", [P, 3 * P])
        ONES = sb("ones", [P, 2])
        SM = sb("small", [P, 80])
        SC = sb("scratch", [P, 11264])
        DESTI, NBI, OEI = SM[:, 24:32].bitcast(I32), SM[0:1, 32:34].bitcast(I32), SM[0:1, 40:48].bitcast(I32)
        ident, tri, iota = TAB[:, 0:P], TAB[:, P:2 * P], TAB[:, 2 * P:3 * P]
        cT, eps, ss, rstd = SM[:, 0:8], SM[:, 8:9], SM[:, 9:13], SM[:, 13:17]
        qn, kn_g, subln, nlam = SM[:, 17:18], SM[:, 18:19], SM[:, 19:20], SM[:, 20:21]
        credit = SM[:, 21:22]
        st8a, st8b = SM[:, 24:40], SM[:, 40:56]
        att = SM[:, 56:72]
        so, sd_o = SM[:, 72:76], SM[:, 76:80]
        sdv, lam_s = so, cT[:, 0:4]

        def sc(at, n):
            return SC[:, at:at + n]

        qkT = sc(0, 2048).rearrange("p (j t) -> p j t", j=4)
        V1 = sc(2048, 2048).rearrange("p (t v) -> p t v", t=TT)
        QKR = sc(4096, 1024).rearrange("p (b n) -> p b n", b=2)
        SG = sc(4096, 1024).rearrange("p (b n) -> p b n", b=2)
        ST = sc(5120, 1280)
        ROT = sc(5120, 1024).rearrange("p (b n) -> p b n", b=2)
        TMP = sc(5120, 1024).rearrange("p (b n) -> p b n", b=2)
        DEC, GN, ACC1, ROW = sc(6400, 512), sc(6912, 512), [sc(7424, 512), sc(10752, 512)], SC[0:1, 7936:8448]
        GATE = sc(8448, 1024)
        ROWS0 = SC[0:1, 8448:8448 + 4 * 512]
        ROPE = sc(9472, 1024).rearrange("p (s t d) -> p s t d", s=2, t=TT)

        ACC = ctx.enter_context(nc.psum_tensor("acc", [P, 4, 512], F32))
        AUX = ctx.enter_context(nc.psum_tensor("aux", [P, 4, 512], F32))

        ada_rows = nc.dram_tensor("ada_rows", (HALVES, 512), F32, kind="Internal").ap()
        y_rows = nc.dram_tensor("y_rows", (Y_BLOCKS * P, D), F32, kind="Internal").ap()

        raw_arrived = [sem(f"raw_arrived{s}") for s in range(RING)]
        raw_used = sem("raw_used")
        hi_done = sem("hi_done")
        pe_steps = sem("pe_steps")
        started = sem("started")
        table_in, rope_in, cols_in, x_in, c_in = (sem(x) for x in ("table_in", "rope_in", "cols_in", "x_in", "c_in"))
        bias_in, mod_in, gate_in, head_in = (sem(x) for x in ("bias_in", "mod_in", "gate_in", "head_in"))
        lg_in, lam_in = sem("lg_in"), sem("lam_in")
        cact_done, ada_ready, ada_ps = sem("cact_done"), sem("ada_ready"), sem("ada_ps")
        row_ready, row_out = sem("row_ready"), sem("row_out")
        n_rms, n_rows, n_T, n_hi, n_lo = (sem(x) for x in ("n_rms", "n_rows", "n_T", "n_hi", "n_lo"))
        acc_free = sem("acc_free")
        rot_done, qk_T, qk_out = sem("rot_done"), sem("qk_T"), sem("qk_out")
        st_ps, st_done = sem("st_ps"), sem("st_done")
        pv_ps, o_rms, o_norm = sem("pv_ps"), sem("o_rms"), sem("o_norm")
        silu_done, y_done, y_T, y_hi, y_lo = (sem(x) for x in ("silu_done", "y_done", "y_T", "y_hi", "y_lo"))
        x_done = sem("x_done")
        out_done = sem("out_done")
        ht_out, lg_ps, lg_exp = sem("ht_out"), sem("lg_ps"), sem("lg_exp")
        cnt_ready, rank_ps, routed, over_set = (sem(x) for x in ("cnt_ready", "rank_ps", "routed", "over_set"))
        pick_ready, picked = sem("pick_ready"), sem("picked")
        xr_done, xt_T, xt_hi, xt_lo = (sem(x) for x in ("xr_done", "xt_T", "xt_hi", "xt_lo"))
        act_g, hid_done, hid_T, hid_hi, hid_lo = (sem(x) for x in ("act_g", "hid_done", "hid_T", "hid_hi", "hid_lo"))
        y_half_a, y_half_v, y_store = sem("y_half_a"), sem("y_half_v"), sem("y_store")
        back_in = [sem(f"back_in{t}") for t in range(TT)]
        back_act = sem("back_act")
        zero_set = sem("zero_set")
        pool_held, sp_held = sem("pool_held"), sem("sp_held")
        a_sq, a_ss, a_rms, a_T, a_kv = (sem(x) for x in ("a_sq", "a_ss", "a_rms", "a_T", "a_kv"))
        ks_in, s_ps, s_max, s_exp = (sem(x) for x in ("ks_in", "s_ps", "s_max", "s_exp"))
        s_a, s_aT, s_at, s_o, s_out = (sem(x) for x in ("s_a", "s_aT", "s_at", "s_o", "s_out"))
        s_root, s_on, s_oT, s_ohi, s_olo = (sem(x) for x in ("s_root", "s_on", "s_oT", "s_ohi", "s_olo"))
        out_free = sem("out_free")
        lam_sum, lam_exp = sem("lam_sum"), sem("lam_exp")
        own = {e: sem(f"own_{e}") for e in ("act", "dve", "pool")}

        def hold(pool, s, value):
            pool.wait_ge(s, value)
            pool.sem_inc(pool_held, 1)

        class Own:

            def __init__(self, eng, name):
                self.eng, self.sem, self.base, self.n = eng, own[name], 0, 0
                self.pool = name == "pool"

            def step(self, ins):
                self.n += 1
                ins.then_inc(self.sem, 1)
                self.eng.wait_ge(self.sem, self.base + self.n)
                if self.pool:
                    self.eng.sem_inc(pool_held, 1)

            def enter(self, i, per):
                self.saved = (self.base + self.n, per)
                self.base, self.n = i * per + self.saved[0], 0

            def leave(self, times):
                at, per = self.saved
                assert self.n == per, (self.n, per)
                self.base, self.n = at + times * per, 0

        C_HEAD = PRE_CHUNKS
        C_MOE0 = C_HEAD + RH * HEAD_CHUNKS
        S_MOE0 = RH * HEAD_SPLIT

        def moe_c(layer, n0):
            return C_MOE0 if layer == 0 else n0 * MOE_CHUNKS + (C_MOE0 + MIX_CHUNKS)

        def moe_s(layer, n0):
            return S_MOE0 if layer == 0 else n0 * MOE_CHUNKS + (S_MOE0 + MIX_CHUNKS)

        def moe_arrived(layer, n0, slot):
            at = C_MOE0 // RING
            return at if layer == 0 else n0 * (MOE_CHUNKS // RING) + (at + [7, 5, 4, 0][slot])

        def load_chunk(eng, slot, src, kt, used):
            if used is not None:
                eng.wait_ge(raw_used, used)
                eng.sem_inc(sp_held, 1)
            eng.dma_start(RAW[:, slot, :].rearrange("p (k n) -> p k n", k=kt), src).then_inc(raw_arrived[slot], 16)

        def split_hi(eng, rslot, wslot, arrived, steps):
            eng.wait_ge(raw_arrived[rslot], 16 * arrived)
            if steps is not None:
                eng.wait_ge(pe_steps, steps)
            eng.activation(WH[:, wslot, :], RAW[:, rslot, :], ACT.Copy).then_inc(hi_done, 1)

        def split_lo(eng, rslot, wslot, arrived, steps, hi):
            eng.wait_ge(raw_arrived[rslot], 16 * arrived)
            if steps is not None:
                eng.wait_ge(pe_steps, steps)
            eng.wait_ge(hi_done, hi)
            eng.tensor_tensor(WL[:, wslot, :], RAW[:, rslot, :], WH[:, wslot, :].bitcast(F32),
                              ALU.subtract).then_inc(raw_used, 1)

        def mm3(out_ap, ah, al, wh, wl, first, last):
            nc.tensor.matmul(out_ap, ah, wh, start=first, stop=False)
            nc.tensor.matmul(out_ap, ah, wl, start=False, stop=False)
            return nc.tensor.matmul(out_ap, al, wh, start=False, stop=last)

        def norm_views(n):
            if n in (0, 1, 4):
                return dict(HR=sc(0, 2048), S=sc(2048, 1024), B=sc(3072, 1024), G=sc(4096, 1024),
                            J=sc(5120, 1024) if n == 0 else sc(6400, 1024))
            if n == 2:
                return dict(HR=sc(6144, 2048), S=sc(4096, 1024), B=sc(5120, 1024), G=sc(6144, 1024), J=BH[:, 0:1024])
            return dict(HR=sc(8192, 2048), S=RAW[:, 3, 0:1024], B=RAW[:, 3, 1024:2048], G=sc(8192, 1024))

        NORM_ROWS = [0, 3, 6, 8, 11]
        NORM_GAIN = [io["norm_mix"][0:1, :], io["norm_ffn"][0:1, :], io["kv_norm"].rearrange("(a n) -> a n", a=1),
                     io["norm_mix"][1:2, :], io["norm_ffn"][1:2, :]]
        rows2 = ada_rows.rearrange("(v h) n -> v (h n)", h=2)
        X_DONE = {1: 32, 2: 36, 3: 36, 4: 52, 5: 56}
        RMS_BASE = {0: 0, 1: 4, 2: 8, 4: 12}

        def norm_pool(pool, n):
            v = norm_views(n)
            pool.dma_start(v["G"], NORM_GAIN[n].broadcast_to([P, D])).then_inc(mod_in, 16)
            if n == 0:
                hold(pool, row_out, 64)
            pool.dma_start(v["S"], rows2[NORM_ROWS[n] + 1:NORM_ROWS[n] + 2, :].broadcast_to([P, D])).then_inc(mod_in, 16)
            pool.dma_start(v["B"], rows2[NORM_ROWS[n]:NORM_ROWS[n] + 1, :].broadcast_to([P, D])).then_inc(mod_in, 16)

        def norm_act_stats(act, n, o):
            for t in range(TT):
                norm_act_stat(act, n, t, o)

        def norm_act_stat(act, n, t, o):
            v = norm_views(n)
            if n == 0:
                act.wait_ge(x_in, 16)
            else:
                act.wait_ge(x_done, X_DONE[n] - TT + t + 1)
            o.step(act.activation(v["J"], X[:, t, :], ACT.Square, accum_out=ss[:, t:t + 1]))
            act.activation(sdv[:, t:t + 1], ss[:, t:t + 1], ACT.Sqrt, bias=eps, scale=1.0 / D).then_inc(n_rms, 1)

        def norm_dve_rows(dve, n, t, o):
            v = norm_views(n)
            if t == 0:
                dve.wait_ge(mod_in, 48 * (n + 1))
                o.step(dve.scalar_tensor_tensor(v["S"], v["S"], 1.0, v["G"], ALU.add, ALU.mult))
            if n != 3:
                dve.wait_ge(n_rms, RMS_BASE[n] + t + 1)
                o.step(dve.reciprocal(rstd[:, t:t + 1], sdv[:, t:t + 1]))
            hr = v["HR"][:, (t % 2) * D:(t % 2 + 1) * D]
            if t >= 2:
                dve.wait_ge(n_T, TT * n + t - 1)
            o.step(dve.scalar_tensor_tensor(hr, X[:, t, :], rstd[:, t:t + 1], v["S"], ALU.mult, ALU.mult))
            dve.tensor_tensor(hr, hr, v["B"], ALU.add).then_inc(n_rows, 1)

        def norm_pe(pe, n, t):
            hr = norm_views(n)["HR"][:, (t % 2) * D:(t % 2 + 1) * D]
            pe.wait_ge(n_rows, TT * n + t + 1)
            if t >= 2:
                if n in (1, 4):
                    pe.wait_ge(ht_out, TT * (n == 4) + t - 1)
                else:
                    pe.wait_ge(n_lo, TT * n + t - 1)
            for k in range(KD):
                q = 2 * (t % 2) + k // 4
                last = nc.tensor.transpose(AUX[:, q, (k % 4) * P:(k % 4 + 1) * P], hr[:, k * P:(k + 1) * P], ident)
            last.then_inc(n_T, 1)

        def aux_pair(t):
            return AUX[:, 2 * (t % 2):2 * (t % 2) + 2, :].rearrange("p a (k c) -> p (a k) c", c=P)

        def norm_act_hi(act, n, tiles=range(TT)):
            for t in tiles:
                act.wait_ge(n_T, TT * n + t + 1)
                act.activation(AH[:, :, t * P:(t + 1) * P], aux_pair(t), ACT.Copy).then_inc(n_hi, 1)

        def norm_dve_lo(dve, n, t):
            dve.wait_ge(n_hi, TT * n + t + 1)
            dve.tensor_tensor(AL[:, :, t * P:(t + 1) * P], aux_pair(t), AH[:, :, t * P:(t + 1) * P].bitcast(F32),
                              ALU.subtract).then_inc(n_lo, 1)

        def norm_dve(dve, n, o, early=0):
            for t in range(TT):
                if t >= early:
                    norm_dve_rows(dve, n, t, o)
                if t:
                    norm_dve_lo(dve, n, t - 1)
            norm_dve_lo(dve, n, TT - 1)

        def ada_acc(dve, o, q, buf, slots, arrived):
            for m in range(2):
                dve.wait_ge(raw_arrived[slots[m]], arrived[m] * 16)
                for k in range(4):
                    w = RAW[:, slots[m], k * 512:(k + 1) * 512]
                    s = cT[:, 4 * m + k:4 * m + k + 1]
                    if m == 0 and k == 0:
                        if not isinstance(q, int) or q >= 2:
                            dve.wait_ge(ada_ps, q + (-1))
                        o.step(dve.tensor_scalar(ACC1[buf], w, s, None, ALU.mult))
                    else:
                        o.step(dve.scalar_tensor_tensor(ACC1[buf], w, s, ACC1[buf], ALU.mult, ALU.add))
                dve.sem_inc(raw_used, 1)
            dve.sem_inc(ada_ready, 1)

        def ada_sum(pe, q, buf):
            pe.wait_ge(ada_ready, q + 1)
            pe.wait_ge(row_ready, q)
            nc.tensor.matmul(AUX[0:1, 3, :], ONES[:, 0:1], ACC1[buf], start=True, stop=True).then_inc(ada_ps, 1)

        def ada_row(dve, q):
            first = isinstance(q, int)
            bias = ROWS0[:, q * 512:(q + 1) * 512] if first else ROW
            dve.wait_ge(ada_ps, q + 1)
            dve.wait_ge(bias_in, 64 if first else (q + 1) * 16)
            dve.tensor_tensor(bias, AUX[0:1, 3, :], bias, ALU.add).then_inc(row_ready, 1)

        def ada_store(pool, q, bias, flat):
            hold(pool, row_out, q * 16)
            pool.dma_start(ROW, bias).then_inc(bias_in, 16)
            hold(pool, row_ready, q + 1)
            pool.dma_start(ada_rows[flat, :], ROW).then_inc(row_out, 16)

        def head_half(h, j):
            if j < 2:
                col, flat = h * 1024 + (2048 + 512 * j), h * 2 + (4 + j)
                return io["ada_w"][0:1, :, ds(col, 512)], io["ada_b"][0:1, ds(col, 512)], ds(flat, 1)
            if j == 2:
                return (io["kv_ada_w"].rearrange("(o k) n -> o k n", o=1)[:, :, ds(h * 512, 512)],
                        io["kv_ada_b"].rearrange("(o n) -> o n", o=1)[:, ds(h * 512, 512)], ds(h + 12, 1))
            col = h * 1536 + 512 * (j - 3)
            return io["ada_w"][1:2, :, ds(col, 512)], io["ada_b"][1:2, ds(col, 512)], ds(h * 3 + (16 + j - 3), 1)

        def k_rows(w, kt, q):
            return w[:, q * kt * P:(q + 1) * kt * P, :].rearrange("o (k p) n -> p (o k) n", p=P)

        def head_pos(h, i):
            return (h * HEAD_CHUNKS + (C_HEAD + i), i % RING, h * (HEAD_CHUNKS // RING) + (C_HEAD // RING + i // RING + 1))

        def free_steps(S):
            return S * 4 + 4

        def fin(S, t=3):
            return S * 4 + (17 + t)

        def after_head(h):
            return (h * (HEAD_CHUNKS // RING) + (C_HEAD + HEAD_CHUNKS) // RING + 1,
                    h * (4 * HEAD_SPLIT) + (4 * HEAD_SPLIT + 4), h * HEAD_SPLIT + (HEAD_SPLIT + 1))

        AT_SPLIT = [HEAD_ORDER.index(x) for x in range(8)]
        AT_ADA = [[i for i, x in enumerate(HEAD_ORDER) if x == "a"][2 * j:2 * j + 2] for j in range(6)]

        def normed(pe, n):
            for t in range(TT - 1):
                norm_pe(pe, n, t)

            def before(t):
                if t == 1:
                    norm_pe(pe, n, TT - 1)
                pe.wait_ge(n_lo, TT * n + t + 1)
            return before

        def project(pe, S0, C0s, w, ah, al, between=None, halves=1, before=None):
            for q in range(2):
                pe.wait_ge(raw_used, C0s[q] + 5)
                slot = (S0[1] + q) % RING
                for t in range(TT):
                    if q == 0:
                        if before:
                            before(t)
                        pe.wait_ge(acc_free, w * 4 + (t + 1))
                    if halves == 2:
                        o, ks, n = ACC[:, t, q * 256:(q + 1) * 256], range(KD), 256
                    else:
                        o, ks, n = ACC[:, t, :], range(4), 512
                    for k in ks:
                        kt = k if halves == 2 else 4 * q + k
                        last = mm3(o, ah(kt, t), al(kt, t), WH[:, slot, k * n:(k + 1) * n], WL[:, slot, k * n:(k + 1) * n],
                                   first=(k == 0 and (q == 0 or halves == 2)),
                                   last=(k == ks[-1] and (q == 1 or halves == 2)))
                    last.then_inc(pe_steps, 1)
                    if between:
                        between(q, t)

        def out_project(pe, S0, C0, w, q, ready):
            pe.wait_ge(raw_used, C0 + 5)
            for t in range(TT):
                if ready:
                    ready(t)
                pe.wait_ge(acc_free, w * 4 + (t + 1))
                for k in range(4):
                    lhs = slice(k * T + t * P, k * T + (t + 1) * P)
                    last = mm3(ACC[:, t, :], BH[:, lhs], BL[:, lhs], WH[:, S0 % RING, k * 512:(k + 1) * 512],
                               WL[:, S0 % RING, k * 512:(k + 1) * 512], first=(k == 0), last=(k == 3))
                last.then_inc(pe_steps, 1)

        def hT(A):
            return lambda kt, t: A[:, kt, t * P:(t + 1) * P]

        XTH, HTH = BH[:, 0:1024], BH[:, 1024:2048]
        XTL, HTL = BL[:, 0:1024], BL[:, 1024:2048]
        SIL, HID, YS, XR = (sc(1024 * i, 1024) for i in range(4))
        rows_hi = AH[:, :, :].rearrange("p a b -> p (a b)").rearrange("p (t d) -> p t d", t=TT)
        rows_lo = AL[:, :, :].rearrange("p a b -> p (a b)").rearrange("p (t d) -> p t d", t=TT)
        W_NAME = ["moe_w1", "moe_w3", "moe_w2"]

        def expert_load(sp, layer, c0, b, expert, first):
            for m in range(MOE_CHUNKS):
                src = io[W_NAME[m // 4]][layer:layer + 1, ds(expert, 1), (m % 4) * 256:(m % 4 + 1) * 256, :]
                used = b * MOE_CHUNKS + c0 + (m + 1)
                if first and layer == 1 and m < RING:
                    used = c0 + 4
                    if m == 1:
                        sp.wait_ge(out_free, 3)
                    if m == 3:
                        sp.wait_ge(x_done, X_DONE[4])
                load_chunk(sp, m % RING, src.rearrange("o e (k p) n -> p (o e k) n", p=P), 2, used)

        def pick_tokens(pe, g, n):
            if n == 0:
                pe.wait_ge(pick_ready, g + 1)
            for t in range(TT):
                for part, rows in enumerate((rows_hi, rows_lo)):
                    last = nc.tensor.matmul(AUX[:, n, :], PT[:, t, :], rows[:, t, n * 512:(n + 1) * 512],
                                            start=(t == 0 and part == 0), stop=(t == TT - 1 and part == 1))
            last.then_inc(picked, 1)

        def transpose_tokens(pe, g):
            for k in range(KD):
                if k % 4 == 0:
                    pe.wait_ge(xr_done, g * 2 + (k // 4 + 1))
                last = nc.tensor.transpose(AUX[:, 2 + k // 4, (k % 4) * P:(k % 4 + 1) * P], XR[:, k * P:(k + 1) * P], ident)
            last.then_inc(xt_T, 1)

        def expert_pe(pe, layer, c0, s0, b, B):
            g = B + layer
            def mms(m, x_hi, x_lo, bank):
                pe.wait_ge(raw_used, b * MOE_CHUNKS + c0 + (m + 5))
                for n in range(2):
                    if m == 8 and n == 1:
                        pe.wait_ge(hid_lo, B * 2 + 2)
                    for k in range(2):
                        kt = 2 * (m % 4) + k
                        at = k * 1024 + n * 512
                        last = mm3(ACC[:, bank + n, :], x_hi[:, kt * P:(kt + 1) * P], x_lo[:, kt * P:(kt + 1) * P],
                                   WH[:, m % RING, at:at + 512], WL[:, m % RING, at:at + 512],
                                   first=(kt == 0), last=(kt == KD - 1))
                last.then_inc(pe_steps, 4)
            pe.wait_ge(xt_hi, g + 1)
            pe.wait_ge(xt_lo, g + 1)
            for m in range(4):
                mms(m, XTH, XTL, 0)
            if not isinstance(B, int):
                pe.wait_ge(y_half_a, B)
                pe.wait_ge(y_half_v, B)
            for m in range(4, 8):
                mms(m, XTH, XTL, 2)
            pick_tokens(pe, g + 1, 0)
            pick_tokens(pe, g + 1, 1)
            pe.wait_ge(hid_done, B + 1)
            for k in range(KD):
                last = nc.tensor.transpose(ACC[:, 2 + k // 4, (k % 4) * P:(k % 4 + 1) * P], HID[:, k * P:(k + 1) * P], ident)
                if k % 4 == 3:
                    last.then_inc(hid_T, 1)
            transpose_tokens(pe, g + 1)
            pe.wait_ge(hid_lo, B * 2 + 1)
            for m in range(8, 12):
                mms(m, HTH, HTL, 2)

        up_pair = ACC[:, 2:4, :].rearrange("p a n -> p (a n)")
        gate_pair = ACC[:, 0:2, :].rearrange("p a n -> p (a n)")

        def y_out_act(act, s_last, B_done):
            act.wait_ge(pe_steps, fin(s_last))
            act.wait_ge(y_store, B_done * 16 + 16 * RH)
            act.activation(YS[:, 0:512], ACC[:, 2, :], ACT.Copy).then_inc(y_half_a, 1)

        def y_out_dve(dve, s_last, B_done):
            dve.wait_ge(pe_steps, fin(s_last))
            dve.wait_ge(y_store, B_done * 16 + 16 * RH)
            dve.tensor_copy(YS[:, 512:1024], ACC[:, 3, :]).then_inc(y_half_v, 1)

        def y_out_pool(pool, layer, b_last, B_done):
            hold(pool, y_half_a, B_done + 1)
            hold(pool, y_half_v, B_done + 1)
            pool.dma_start(y_rows[ds(b_last * P, P), :], YS).then_inc(y_store, 16)

        def token_rows(act, g):
            for n in range(2):
                act.wait_ge(picked, g * 2 + (n + 1))
                act.activation(XR[:, n * 512:(n + 1) * 512], AUX[:, n, :], ACT.Copy).then_inc(xr_done, 1)

        def tokens_hi(act, g):
            act.wait_ge(xt_T, g + 1)
            act.activation(XTH, AUX[:, 2:4, :].rearrange("p a n -> p (a n)"), ACT.Copy).then_inc(xt_hi, 1)

        def tokens_lo(dve, g):
            dve.wait_ge(xt_hi, g + 1)
            dve.tensor_tensor(XTL, AUX[:, 2:4, :].rearrange("p a n -> p (a n)"), XTH.bitcast(F32),
                              ALU.subtract).then_inc(xt_lo, 1)

        def kv_hi(act, n0, m):
            split_hi(act, KV_SLOT[m], m % RING, n0 * 3 + (C_MOE0 // RING + KV_SLOT[:m + 1].count(KV_SLOT[m])), free_steps(moe_s(1, n0) - MIX_CHUNKS + m))

        def kv_lo(dve, n0, m):
            s0 = moe_s(1, n0) - MIX_CHUNKS
            split_lo(dve, KV_SLOT[m], m % RING, n0 * 3 + (C_MOE0 // RING + KV_SLOT[:m + 1].count(KV_SLOT[m])), free_steps(s0 + m), s0 + m + 1)

        def first_hi(act, layer, n0, ms):
            s0 = moe_s(layer, n0)
            for m in ms:
                split_hi(act, m, m, moe_arrived(layer, n0, m) + 1, free_steps(s0 + m))

        def first_lo(dve, layer, n0, ms):
            s0 = moe_s(layer, n0)
            for m in ms:
                split_lo(dve, m, m, moe_arrived(layer, n0, m) + 1, free_steps(s0 + m), s0 + (m + 1))

        def expert_act(act, layer, n0, s0, b, B, first):
            def hi(m):
                split_hi(act, m % RING, m % RING, b * 3 + moe_arrived(layer, n0, m % RING) + (m // RING + 1),
                         free_steps(b * MOE_CHUNKS + s0 + m))
            if not first:
                for m in range(3):
                    hi(m)
                y_out_act(act, b * MOE_CHUNKS + s0 - 1, B - 1)
            for m in range(RING if first else 3, 7):
                hi(m)
            act.wait_ge(pe_steps, fin(b * MOE_CHUNKS + s0 + 3))
            act.activation(SIL, gate_pair, ACT.Silu).then_inc(act_g, 1)
            for m in range(7, 11):
                hi(m)
            token_rows(act, B + (layer + 1))
            for a in range(2):
                act.wait_ge(hid_T, B * 2 + (a + 1))
                act.activation(HTH[:, a * 512:(a + 1) * 512], ACC[:, 2 + a, :], ACT.Copy).then_inc(hid_hi, 1)
            hi(11)
            tokens_hi(act, B + (layer + 1))

        def expert_dve(dve, layer, n0, c0, s0, b, B, first):
            def lo(m):
                split_lo(dve, m % RING, m % RING, b * 3 + moe_arrived(layer, n0, m % RING) + (m // RING + 1),
                         free_steps(b * MOE_CHUNKS + s0 + m), b * MOE_CHUNKS + s0 + (m + 1))
            if not first:
                for m in range(3):
                    lo(m)
                y_out_dve(dve, b * MOE_CHUNKS + s0 - 1, B - 1)
            for m in range(RING if first else 3, 10):
                lo(m)
            dve.wait_ge(pe_steps, fin(b * MOE_CHUNKS + s0 + 7))
            dve.wait_ge(act_g, B + 1)
            dve.tensor_tensor(HID, up_pair, SIL, ALU.mult).then_inc(hid_done, 1)
            lo(10)
            for a in range(2):
                half = slice(a * 512, (a + 1) * 512)
                dve.wait_ge(hid_hi, B * 2 + (a + 1))
                dve.tensor_tensor(HTL[:, half], ACC[:, 2 + a, :], HTH[:, half].bitcast(F32), ALU.subtract).then_inc(hid_lo, 1)
            lo(11)
            tokens_lo(dve, B + (layer + 1))

        R0 = 9472
        at = [R0]

        def small(n, inner=None):
            v = SC[:, at[0]:at[0] + n]
            at[0] += n
            return v if inner is None else v.rearrange("p (a b) -> p a b", b=inner)

        LG, EX, EXR = small(80, 20), small(20), small(20)
        GM, GS, GT, BEST, M1, M2, WB = (small(4) for _ in range(7))
        RV4, RV16, E128, ADJ, OB, OST = small(4), small(16), small(16), small(16), small(16), small(16)
        GA, OG = small(16, 4), small(16, 4)
        EL, EA, O1, O2, CN, DS1 = (small(64, 16) for _ in range(6))
        CS = [small(24), small(24)]
        WTS, DEST, DD = small(8, 4), small(8, 4), small(8, 4)
        OVX, OVE = small(8 * 16, 16), small(8)
        BR = small(20)
        assert at[0] <= 10240 + 200, at
        WR = sc(7424, 160).rearrange("p (k n) -> p k n", n=20)
        HTF = sc(5120, 1024).rearrange("p (k c) -> p k c", c=P)
        PICKA, PICKB, PICKD = sc(10500, 128), sc(10628, 512), sc(7744, 128)
        BEFORE, RANK = sc(7600, 80).rearrange("p (t e) -> p t e", e=NE), sc(7680, 64).rearrange("p (t e) -> p t e", e=NE)

        def col(v, n):
            return v.rearrange("p (a o) -> p a o", o=1).broadcast_to([P, v.shape[1], n])

        def row(v, a, parts=P):
            return v.rearrange("p (o n) -> p o n", o=1).broadcast_to([parts, a, v.shape[1]])

        def moe_norm_act(act, n, o):
            layer = int(n == 4)
            norm_act_stats(act, n, o)
            def rows(t):
                act.wait_ge(n_rows, TT * n + t + 1)
                hr = norm_views(n)["HR"][:, (t % 2) * D:(t % 2 + 1) * D]
                act.activation(rows_hi[:, t, :], hr, ACT.Copy).then_inc(n_hi, 1)
            for t in range(TT):
                rows(t)
                act.wait_ge(n_T, TT * n + t + 1)
                act.wait_ge(lg_ps, TT * layer + t)
                act.activation(HTF, aux_pair(t), ACT.Copy).then_inc(ht_out, 1)

        def moe_norm_dve(dve, n, o):
            def lo(t):
                dve.wait_ge(n_hi, TT * n + t + 1)
                hr = norm_views(n)["HR"][:, (t % 2) * D:(t % 2 + 1) * D]
                o.step(dve.tensor_tensor(rows_lo[:, t, :], hr, rows_hi[:, t, :].bitcast(F32), ALU.subtract))
                dve.sem_inc(n_lo, 1)
            for t in range(TT):
                norm_dve_rows(dve, n, t, o)
                if t:
                    lo(t - 1)
            lo(TT - 1)

        def moe_norm_pe(pe, n):
            layer = int(n == 4)
            def logits(t):
                pe.wait_ge(ht_out, TT * layer + t + 1)
                if t == 0:
                    pe.wait_ge(lg_in, 64 * (layer + 1))
                for k in range(KD):
                    last = nc.tensor.matmul(ACC[:, 3, t * 20:(t + 1) * 20], HTF[:, k, :], WR[:, k, :],
                                            start=(k == 0), stop=(k == KD - 1))
                last.then_inc(lg_ps, 1)
            norm_pe(pe, n, 0)
            for t in range(1, TT):
                norm_pe(pe, n, t)
                logits(t - 1)
            logits(TT - 1)

        def route_dve(dve, layer, o):
            st = o.step
            st(dve.tensor_scalar(RV4, iota[:, 0:NG], -1.0, float(NG), ALU.mult, ALU.add))
            st(dve.tensor_scalar(RV16, iota[:, 0:NE], -1.0, float(NE), ALU.mult, ALU.add))
            st(dve.tensor_scalar(E128, iota[:, 0:NE], float(P), None, ALU.mult))
            st(dve.memset(BEFORE[:, 0, :], 0.0))
            st(dve.memset(CS[0], 0.0))
            st(dve.memset(CS[1], 0.0))
            dve.wait_ge(lg_ps, TT * (layer + 1))
            st(dve.tensor_tensor(LG, ACC[:, 3, 0:80].rearrange("p (t n) -> p t n", n=20), row(BR, TT), ALU.add))
            gl, el = LG[:, :, 0:NG], LG[:, :, NG:20]
            st(dve.tensor_reduce(GM, gl, AX.X, ALU.max))
            exg = EX[:, 0:16].rearrange("p (a b) -> p a b", b=4)
            st(dve.tensor_tensor(exg, gl, col(GM, NG), ALU.subtract))
            st(dve.tensor_tensor(GA, gl, col(GM, NG), ALU.is_equal))
            st(dve.tensor_tensor(GA, GA, row(RV4, TT), ALU.mult))
            st(dve.tensor_reduce(BEST, GA, AX.X, ALU.max))
            st(dve.tensor_tensor(OG, row(RV4, TT), col(BEST, NG), ALU.is_equal))
            st(dve.tensor_scalar(OG, OG, -1.0, BIG, ALU.add, ALU.mult))
            og4 = OG.rearrange("p t (g o) -> p t g o", o=1).broadcast_to([P, TT, NG, EPG])
            st(dve.tensor_tensor(EL.rearrange("p t (g e) -> p t g e", e=EPG), el.rearrange("p t (g e) -> p t g e", e=EPG),
                                 og4, ALU.add))

            def top(m, one):
                st(dve.tensor_reduce(m, EL, AX.X, ALU.max))
                st(dve.tensor_tensor(EA, EL, col(m, NE), ALU.is_equal))
                st(dve.tensor_tensor(EA, EA, row(RV16, TT), ALU.mult))
                st(dve.tensor_reduce(BEST, EA, AX.X, ALU.max))
                st(dve.tensor_tensor(one, row(RV16, TT), col(BEST, NE), ALU.is_equal))
            top(M1, O1)
            st(dve.scalar_tensor_tensor(EL, O1, -3.0 * BIG, EL, ALU.mult, ALU.add))
            top(M2, O2)
            st(dve.tensor_tensor(EX[:, 16:20], M2, M1, ALU.subtract))
            st(dve.tensor_tensor(CN, O1, O2, ALU.add))
            dve.sem_inc(cnt_ready, 1)
            dve.wait_ge(rank_ps, layer + 1)
            for t in range(TT):
                st(dve.tensor_tensor(BEFORE[:, t + 1, :], BEFORE[:, t, :], AUX[:, 1, t * NE:(t + 1) * NE], ALU.add))
            tot = BEFORE[:, TT, :]
            st(dve.tensor_scalar(OB, tot, float(P), None, ALU.is_gt))
            st(dve.scalar_tensor_tensor(OB, tot, 2.0 * P, OB, ALU.is_gt, ALU.add))
            st(dve.scalar_tensor_tensor(OB, tot, 3.0 * P, OB, ALU.is_gt, ALU.add))
            st(dve.tensor_copy(CS[0][:, 8:24], OB))
            for i, s in enumerate((1, 2, 4, 8)):
                a, b = CS[i % 2], CS[1 - i % 2]
                st(dve.tensor_tensor(b[:, 8:24], a[:, 8:24], a[:, 8 - s:24 - s], ALU.add))
            oend = CS[0][:, 8:24]
            st(dve.tensor_tensor(OST, oend, OB, ALU.subtract))
            rank = RANK
            st(dve.tensor_tensor(rank, AUX[:, 0, 0:64].rearrange("p (t e) -> p t e", e=NE), BEFORE[:, 0:TT, :], ALU.add))
            st(dve.scalar_tensor_tensor(ADJ, OST, float(P), E128, ALU.mult, ALU.subtract))
            st(dve.tensor_scalar(ADJ, ADJ, float((NE - 1) * P), None, ALU.add))
            st(dve.tensor_scalar(EA, rank, float(P), None, ALU.is_ge))
            st(dve.tensor_tensor(EA, EA, row(ADJ, TT), ALU.mult))
            st(dve.tensor_tensor(DS1, rank, row(E128, TT), ALU.add))
            st(dve.tensor_tensor(DS1, DS1, EA, ALU.add))
            for k, one in enumerate((O1, O2)):
                st(dve.tensor_tensor(EA, one, DS1, ALU.mult))
                st(dve.tensor_reduce(DEST[:, k, :], EA, AX.X, ALU.add))
            dve.sem_inc(routed, 1)

        def route_rest_dve(dve, layer, o):
            st = o.step
            oend = CS[0][:, 8:24]
            st(dve.tensor_copy(NBI[0:1, layer:layer + 1], oend[0:1, 15:16]))
            ov = OVX[0:1, 0:MAX_OVER, :]
            it = iota[0:1, 0:MAX_OVER].rearrange("p (a o) -> p a o", o=1).broadcast_to([1, MAX_OVER, NE])
            st(dve.tensor_tensor(ov, row(oend[0:1, :], MAX_OVER, 1), it, ALU.is_le))
            st(dve.tensor_reduce(OVE[0:1, 0:MAX_OVER], ov, AX.X, ALU.add))
            st(dve.tensor_scalar(OVE[0:1, 0:MAX_OVER], OVE[0:1, 0:MAX_OVER], float(NE - 1), None, ALU.min))
            st(dve.tensor_copy(OEI[0:1, 0:MAX_OVER], OVE[0:1, 0:MAX_OVER]))
            dve.sem_inc(over_set, 1)
            st(dve.tensor_copy(DESTI, DEST.rearrange("p a b -> p (a b)")))
            dve.wait_ge(lg_exp, layer + 1)
            st(dve.tensor_reduce(GS, EXR[:, 0:16].rearrange("p (a b) -> p a b", b=4), AX.X, ALU.add))
            st(dve.tensor_scalar(WB, EXR[:, 16:20], 1.0, None, ALU.add))
            st(dve.tensor_tensor(GT, GS, WB, ALU.mult))
            st(dve.reciprocal(WTS[:, 0, :], GT))
            st(dve.tensor_tensor(WTS[:, 1, :], WTS[:, 0, :], EXR[:, 16:20], ALU.mult))

        def route_act(act, layer):
            act.wait_ge(cnt_ready, layer + 1)
            act.activation(EXR, EX, ACT.Exp).then_inc(lg_exp, 1)

        def route_pe(pe, layer):
            pe.wait_ge(cnt_ready, layer + 1)
            counts = CN.rearrange("p t e -> p (t e)")
            nc.tensor.matmul(AUX[:, 0, 0:TT * NE], tri, counts, start=True, stop=True)
            nc.tensor.matmul(AUX[:, 1, 0:TT * NE], ONES[:, 0:1].to_broadcast([P, P]), counts, start=True,
                             stop=True).then_inc(rank_ps, 1)

        def first_pick(dve, o):
            for t in range(TT):
                o.step(dve.tensor_scalar(PICKD, iota, DEST[:, 1, t:t + 1], None, ALU.is_equal))
                o.step(dve.scalar_tensor_tensor(PT[:, t, :], iota, DEST[:, 0, t:t + 1], PICKD, ALU.is_equal, ALU.add))
            dve.sem_inc(pick_ready, 1)

        def build_pick(pool, g, o):
            st = o.step
            hold(pool, picked, g * 2)
            for t in range(TT):
                st(pool.tensor_scalar(PICKB[:, t * P:(t + 1) * P], iota, DD[:, 1, t:t + 1], None, ALU.is_equal))
                st(pool.tensor_scalar(PICKA, iota, DD[:, 0, t:t + 1], None, ALU.is_equal))
                st(pool.tensor_tensor(PT[:, t, :], PICKA, PICKB[:, t * P:(t + 1) * P], ALU.add))
            st(pool.tensor_scalar(DD.rearrange("p a b -> p (a b)"), DD.rearrange("p a b -> p (a b)"),
                                  -float(P), None, ALU.add))
            pool.sem_inc(pick_ready, 1)
        PICK_STEPS = 13

        def blocks(eng, layer, n0, body, own_steps=None):
            base = 0 if layer == 0 else n0
            body(0, base, True)
            with eng.Fori(1, NE) as b:
                if own_steps:
                    own_steps[0].enter(b - 1, own_steps[1])
                body(b, b + base, False)
                if own_steps:
                    own_steps[0].leave(NE - 1)
            eng.wait_ge(over_set, layer + 1)
            n_over = eng.value_load(NBI[0:1, layer:layer + 1], min_val=0, max_val=MAX_OVER)
            with eng.Fori(0, MAX_OVER) as i:
                with eng.If(i < n_over):
                    if own_steps:
                        own_steps[0].enter(i, own_steps[1])
                    body(i + NE, i + NE + base, False)
                    if own_steps:
                        own_steps[0].leave(n_over)
            return n_over + NE, n_over + (NE + base)

        def back(layer, t):
            s = t if layer else t % 2
            return sc(2 * D * s, D), sc(2 * D * s + D, D)

        def combine_pool(pool, layer, N):
            hold(pool, y_store, N * 16 + 16 * RH)
            for t in range(TT):
                if t >= 2 and layer == 0:
                    hold(pool, x_done, X_DONE[2] - TT + t - 1)
                for k in range(2):
                    pool.indirect_dma_start(
                        out=back(layer, t)[k], out_offset=None, in_=y_rows,
                        in_offset=bass.IndirectOffsetOnAxis(ap=DESTI[:, k * TT + t:k * TT + t + 1], axis=0),
                    ).then_inc(back_in[t], 16)

        def combine_act(act, layer, o):
            for t in range(TT):
                act.wait_ge(back_in[t], 32 * (layer + 1))
                y1 = back(layer, t)[0]
                act.activation(y1, y1, ACT.Copy, scale=WTS[:, 0, t:t + 1]).then_inc(back_act, 1)
                if layer == 0:
                    if t >= 1:
                        norm_act_stat(act, 2, t - 1, o)
                    if t >= 2:
                        norm_act_hi(act, 2, [t - 2])
            if layer == 0:
                norm_act_stat(act, 2, TT - 1, o)
                norm_act_hi(act, 2, [TT - 2, TT - 1])

        def combine_dve(dve, layer, o, gate_count):
            dve.wait_ge(gate_in, 16 * gate_count)
            for t in range(TT):
                y1, y2 = back(layer, t)
                dve.wait_ge(back_in[t], 32 * (layer + 1))
                dve.wait_ge(back_act, TT * layer + t + 1)
                o.step(dve.scalar_tensor_tensor(y2, y2, WTS[:, 1, t:t + 1], y1, ALU.mult, ALU.add))
                o.step(dve.tensor_tensor(y2, y2, GATE, ALU.mult))
                dve.tensor_tensor(X[:, t, :], X[:, t, :], y2, ALU.add).then_inc(x_done, 1)
                if layer == 0:
                    if t >= 1:
                        norm_dve_rows(dve, 2, t - 1, o)
                    if t >= 2:
                        norm_dve_lo(dve, 2, t - 2)
            if layer == 0:
                norm_dve_rows(dve, 2, TT - 1, o)
                norm_dve_lo(dve, 2, TT - 2)
                norm_dve_lo(dve, 2, TT - 1)

        KT = sc(0, 4096).rearrange("p (h t) -> p h t", h=AHEADS)
        VV = sc(4096, 4096).rearrange("p (t n) -> p t n", t=TT)
        QT = sc(8192, 2048).rearrange("p (h t) -> p h t", h=4)
        KS = [sc(10240, 512), sc(10752, 512)]
        JUNK = PT[:, 0, :]
        OUT = RAW[:, 2, :].rearrange("p (t j v) -> p t j v", t=TT, v=P)
        ON = RAW[:, 3, 1024:2048].rearrange("p (b j v) -> p b j v", b=2, v=P)
        out_ms, out_rms = st8a, st8b
        SQ = RAW[:, 3, 0:1024].rearrange("p (b n) -> p b n", b=2)
        KN = RAW[:, 3, 1024:2048].rearrange("p (b n) -> p b n", b=2)
        EE = [RAW[:, 3, 0:1024], RAW[:, 3, 1024:2048], RAW[:, 1, 0:1024]]
        EE = [e.rearrange("p (t n) -> p t n", t=2) for e in EE]
        GATE2, TMP2 = RAW[:, 3, 0:1024], RAW[:, 3, 1024:2048].rearrange("p (b n) -> p b n", b=2)

        def qk_norm_act(act, z, w, S, gain, dst, x_wait):
            def sq(t):
                act.wait_ge(pe_steps, fin(S, t))
                if x_wait is not None:
                    act.wait_ge(x_done, x_wait)
                if t >= 2:
                    act.wait_ge(a_ss, z * 4 + (t - 1))
                act.activation(SQ[:, t % 2, :], ACC[:, t, :], ACT.Square).then_inc(a_sq, 1)

            def root(t):
                act.wait_ge(a_ss, z * 4 + (t + 1))
                act.activation(st8b[:, 8 * (t % 2):8 * (t % 2) + 8], st8a[:, 8 * (t % 2):8 * (t % 2) + 8], ACT.Sqrt,
                               bias=eps, scale=1.0 / HD).then_inc(a_rms, 1)

            def out_T(t):
                act.wait_ge(a_T, z * 4 + (t + 1))
                act.activation(dst(t), AUX[:, t % 2, :].rearrange("p (h c) -> p h c", c=P), ACT.Copy,
                               scale=gain).then_inc(a_kv, 1)
            sq(0)
            for t in range(1, TT + 1):
                if t < TT:
                    sq(t)
                root(t - 1)
                if t >= 2:
                    out_T(t - 2)
            out_T(TT - 1)

        def qk_norm_dve(dve, z, o):
            def ab(t):
                return st8a[:, 8 * (t % 2):8 * (t % 2) + 8], st8b[:, 8 * (t % 2):8 * (t % 2) + 8]

            def sums(t):
                dve.wait_ge(a_sq, z * 4 + (t + 1))
                dve.tensor_reduce(ab(t)[0], SQ[:, t % 2, :].rearrange("p (g d) -> p g d", d=HD), AX.X, ALU.add).then_inc(a_ss, 1)

            sums(0)
            for t in range(TT):
                if t + 1 < TT:
                    sums(t + 1)
                dve.wait_ge(a_rms, z * 4 + (t + 1))
                b = ab(t)[1]
                o.step(dve.reciprocal(b, b))
                if t >= 2:
                    dve.wait_ge(a_T, z * 4 + (t - 1))
                dve.tensor_tensor(KN[:, t % 2, :].rearrange("p (g d) -> p g d", d=HD),
                                  ACC[:, t, :].rearrange("p (g d) -> p g d", d=HD),
                                  col(b, HD), ALU.mult).then_inc(acc_free, 1)
        QK_STEPS = TT

        def qk_norm_pe(pe, z, w):
            for t in range(TT):
                pe.wait_ge(acc_free, w * 4 + (4 + t + 1))
                if t >= 2:
                    pe.wait_ge(a_kv, z * 4 + (t - 1))
                for j in range(4):
                    last = nc.tensor.transpose(AUX[:, t % 2, j * P:(j + 1) * P], KN[:, t % 2, j * P:(j + 1) * P], ident)
                last.then_inc(a_T, 1)

        UNITS = [(j, qb) for j in range(4) for qb in range(TT)]

        def mix_pos(g, i):
            arrived = {0: g * 2 + 4, 1: g + 4, 2: g + 3, 3: g * 2 + 5}[i]
            return HALF_SLOT[i], arrived

        qn8 = SM[:, 22:23]
        LAMV, LAMT = sc(10240, 256), sc(10752, HD)
        PV_BANK = {3: 1, 2: 2, 1: 0, 0: 1}
        ST_AT = [0, 512, 896, 1152]

        def head_y_hi(act, h, t):
            act.wait_ge(y_T, h * 4 + (t + 1))
            act.activation(bview(BH)[:, :, t * P:(t + 1) * P], AUX[:, t % 2, :].rearrange("p (k c) -> p k c", c=P),
                           ACT.Copy).then_inc(y_hi, 1)

        def head_y_lo(dve, h, t):
            dve.wait_ge(y_hi, h * 4 + (t + 1))
            dve.tensor_tensor(bview(BL)[:, :, t * P:(t + 1) * P], AUX[:, t % 2, :].rearrange("p (k c) -> p k c", c=P),
                              bview(BH)[:, :, t * P:(t + 1) * P].bitcast(F32), ALU.subtract).then_inc(y_lo, 1)

        def bview(b):
            return b[:, :].rearrange("p (k t) -> p k t", t=T)

        def residual_add(dve, o, steps, q, t, gate, tmp):
            cols = slice(q * 512, (q + 1) * 512)
            dve.wait_ge(pe_steps, steps)
            o.step(dve.tensor_tensor(tmp[:, t % 2, :], ACC[:, t, :], gate[:, cols], ALU.mult))
            dve.sem_inc(acc_free, 1)
            dve.tensor_tensor(X[:, t, cols], X[:, t, cols], tmp[:, t % 2, :], ALU.add).then_inc(x_done, 1)

        block = ctx.enter_context(nc.Block())

        @block.sync
        def _(sp):
            sp.wait_ge(started, 1)
            for m in range(PRE_CHUNKS):
                q = m // 2
                load_chunk(sp, m % RING, k_rows(io["ada_w"][0:1, :, q * 512:(q + 1) * 512], 4, m % 2), 4, m + 1)
                if m == PRE_CHUNKS - 3:
                    sp.dma_start(X[:, :, :], io["x"].rearrange("b (t p) d -> p (b t) d", p=P)).then_inc(x_in, 16)
            with sp.Fori(0, RH) as h:
                for i, what in enumerate(HEAD_ORDER):
                    C, slot, _ = head_pos(h, i)
                    if what == "a":
                        a = sum(x == "a" for x in HEAD_ORDER[:i])
                        load_chunk(sp, slot, k_rows(head_half(h, a // 2)[0], 4, a % 2), 4, C + 1)
                    elif what < 2:
                        load_chunk(sp, slot, k_rows(io["ret_w_in"][0:1, :, ds(h * RK + what * 1024, RK)], 8, 0), 8, C + 1)
                    elif what < 6:
                        col0 = h * RV + (2048 if what < 4 else 4096)
                        load_chunk(sp, slot, k_rows(io["ret_w_in"][0:1, :, ds(col0, RV)], 4, what % 2), 4, C + 1)
                    else:
                        n = (what - 6) * 512
                        load_chunk(sp, slot, k_rows(io["ret_w_out"][0:1, ds(h * RV, RV), n:n + 512], 4, 0), 4, C + 1)
            def experts(layer, n0):
                c0 = moe_c(layer, n0)
                base = 0 if layer == 0 else n0
                expert_load(sp, layer, c0, 0, 0, True)
                with sp.Fori(1, NE) as e:
                    expert_load(sp, layer, c0, e, e, False)
                sp.wait_ge(over_set, layer + 1)
                n_over = sp.value_load(NBI[0:1, layer:layer + 1], min_val=0, max_val=MAX_OVER)
                with sp.Fori(0, MAX_OVER) as i:
                    with sp.If(i < n_over):
                        expert = sp.value_load(OEI[0:1, ds(i, 1)], min_val=0, max_val=NE - 1)
                        expert_load(sp, layer, c0, i + NE, expert, False)
                return n_over + (NE + base)
            n0 = experts(0, None)
            c0 = moe_c(1, n0) - MIX_CHUNKS
            kv = io["kv_w"].rearrange("(o k) n -> o k n", o=1)
            for m in range(8):
                u, q = m // 2, m % 2
                if m == 3:
                    for t in range(TT):
                        sp.wait_ge(back_in[t], 32)
                load_chunk(sp, KV_SLOT[m], k_rows(kv[:, :, u * 512:(u + 1) * 512], 4, q), 4, c0 + (m + 2 if m >= 3 else 4))
            with sp.Fori(0, 2) as g:
                for i in range(4):
                    if i < 2:
                        src = k_rows(io["diff_w_q"][0:1, :, ds(g * 512, 512)], 4, i)
                    else:
                        src = k_rows(io["diff_w_out"][0:1, ds(g * 512, 512), (i - 2) * 512:(i - 1) * 512], 4, 0)
                    if i == 1:
                        sp.wait_ge(out_free, g + 1)
                        sp.sem_inc(sp_held, 1)
                    load_chunk(sp, mix_pos(g, i)[0], src, 4, g * 4 + c0 + (8 + i + 5 - SLOT_BACK[i]))
            experts(1, n0)

        @block.gpsimd
        def _(pool):
            o = Own(pool, "pool")
            pool.dma_start(cT, io["c"].rearrange("b (k p) -> p (b k)", p=P), allow_slow_non_contiguous=True).then_inc(c_in, 16)
            pool.dma_start(TAB[:, :], io["table"]).then_inc(table_in, 16)
            for q in range(4):
                pool.dma_start(ROWS0[:, q * 512:(q + 1) * 512], io["ada_b"][0:1, q * 512:(q + 1) * 512]).then_inc(bias_in, 16)
            for q in range(4):
                hold(pool, row_ready, q + 1)
                pool.dma_start(ada_rows[q:q + 1, :], ROWS0[:, q * 512:(q + 1) * 512]).then_inc(row_out, 16)
            norm_pool(pool, 0)
            pool.dma_start(ROPE[:, 0, :, :], io["rope"][0:1, :, :].rearrange("o (t p) d -> p (o t) d", p=P)).then_inc(rope_in, 16)
            pool.dma_start(ROPE[:, 1, :, :], io["rope"][1:2, :, :].rearrange("o (t p) d -> p (o t) d", p=P)).then_inc(rope_in, 16)
            for i, name in enumerate(("q_norm", "k_norm")):
                v = (io[name] if name == "q_norm" else io[name].rearrange("(o d) -> o d", o=1)).rearrange("o d -> d o")
                for z in range(2):
                    pool.dma_start(SM[z * HD:(z + 1) * HD, 17 + i:18 + i], v, allow_slow_non_contiguous=True).then_inc(cols_in, 16)
            pool.dma_start(subln, io["diff_subln"].rearrange("o d -> d o"), allow_slow_non_contiguous=True).then_inc(cols_in, 16)
            pool.memset(PICKA, 0.0).then_inc(zero_set, 1)
            hold(pool, zero_set, 1)
            with pool.Fori(0, RH) as h:
                pool.dma_start(y_rows[ds(h * 2 * P + NE * P, 2 * P), :].rearrange("(p r) (k c) -> p (r k) c", p=P, c=P),
                               PICKA.rearrange("p (o c) -> p o c", o=1).broadcast_to([P, 16, P])).then_inc(y_store, 16)
                hold(pool, acc_free, h * 20 + 4)
                pool.dma_start(DEC, io["decay"][ds(h, 1), :, :].rearrange("o p n -> p (o n)")).then_inc(head_in, 16)
                pool.dma_start(GN, io["ret_gn"][0:1, ds(h * RV, RV)].broadcast_to([P, RV])).then_inc(head_in, 16)
                for j in range(6):
                    _, bias, flat = head_half(h, j)
                    ada_store(pool, h * 6 + (4 + j), bias, flat)
                    if j == 1:
                        with pool.If(h < 1):
                            hold(pool, row_out, 96)
                            pool.dma_start(GATE, rows2[2:3, :].broadcast_to([P, D])).then_inc(gate_in, 16)
            def moe_prelude(n, gate_row):
                layer = int(n == 4)
                norm_pool(pool, n)
                pool.dma_start(WR[:, :, 0:NG], k_rows(io["moe_w_group"][layer:layer + 1], 8, 0)).then_inc(lg_in, 16)
                pool.dma_start(WR[:, :, NG:20], k_rows(io["moe_w_expert"][layer:layer + 1], 8, 0)).then_inc(lg_in, 16)
                pool.dma_start(BR[:, 0:NG], io["moe_b_group"][layer:layer + 1, :].broadcast_to([P, NG])).then_inc(lg_in, 16)
                pool.dma_start(BR[:, NG:20], io["moe_b_expert"][layer:layer + 1, :].broadcast_to([P, NE])).then_inc(lg_in, 16)
                hold(pool, x_done, X_DONE[n])
                pool.dma_start(GATE, rows2[gate_row:gate_row + 1, :].broadcast_to([P, D])).then_inc(gate_in, 16)

            def moe(layer, n0):
                base = 0 if layer == 0 else n0
                hold(pool, routed, layer + 1)
                o.step(pool.tensor_scalar(DD.rearrange("p a b -> p (a b)"), DEST.rearrange("p a b -> p (a b)"),
                                          -float(P), None, ALU.add))
                if layer == 0:
                    norm_pool(pool, 2)

                def body(b, B, first):
                    build_pick(pool, B + (layer + 1), o)
                    if not first:
                        y_out_pool(pool, layer, b - 1, B - 1)
                n, N = blocks(pool, layer, n0, body, (o, PICK_STEPS))
                y_out_pool(pool, layer, n - 1, N - 1)
                combine_pool(pool, layer, N)
                return N

            hold(pool, row_out, 16 * HALVES)
            hold(pool, y_store, 16 * RH)
            hold(pool, y_lo, 16)
            moe_prelude(1, 5)
            n0 = moe(0, None)
            hold(pool, x_done, X_DONE[2])
            pool.dma_start(LAMV, io["diff_lam"].rearrange("o a d -> o (a d)").broadcast_to([P, 4 * HD])).then_inc(lam_in, 16)
            hold(pool, a_kv, 8)
            norm_pool(pool, 3)
            with pool.Fori(0, 2) as g:
                hold(pool, a_kv, g * 4 + 9)
                for j in range(4):
                    if j >= 2:
                        hold(pool, s_ps, g * 16 + 4 * (j - 1))
                    pool.tensor_copy(KS[j % 2], KT[:, ds(g * 4 + j, 1), :].rearrange("p o t -> p (o t)")).then_inc(ks_in, 1)
                hold(pool, s_o, g * 16 + 16)
                pool.dma_start(GATE2, rows2[10:11, :].broadcast_to([P, D])).then_inc(gate_in, 16)
            hold(pool, s_olo, 2 * TT)
            moe_prelude(4, 13)
            moe(1, n0)
            for t in range(TT):
                hold(pool, x_done, X_DONE[5] - TT + t + 1)
                pool.dma_start(out[0, t * P:(t + 1) * P, :], X[:, t, :]).then_inc(out_done, 16)
            hold(pool, out_done, 16 * TT)

        @block.scalar
        def _(act):
            o = Own(act, "act")
            act.wait_ge(started, 1)
            act.wait_ge(c_in, 16)
            act.activation(cT, cT, ACT.Silu).then_inc(cact_done, 1)
            norm_act_stats(act, 0, o)
            norm_act_hi(act, 0)

            split_hi(act, 0, 0, C_HEAD // RING + 1, 4)
            with act.Fori(0, RH) as h:
                def hi(i):
                    _, slot, arrived = head_pos(h, AT_SPLIT[i])
                    split_hi(act, slot, i % RING, arrived, free_steps(h * HEAD_SPLIT + i))
                o.enter(h, TT)
                for i in range(1, 4):
                    hi(i)
                for t in range(TT):
                    act.wait_ge(qk_T, h * 4 + (t + 1))
                    act.activation(qkT[:, :, t * P:(t + 1) * P], AUX[:, t % 2, :].rearrange("p (j c) -> p j c", c=P),
                                   ACT.Copy).then_inc(qk_out, 1)
                hi(4)
                for t in range(TT):
                    act.wait_ge(pe_steps, fin(h * HEAD_SPLIT + 3, t))
                    act.activation(V1[:, t, :], ACC[:, t, :], ACT.Copy).then_inc(acc_free, 1)
                hi(5)
                for n, t in enumerate(reversed(range(TT))):
                    act.wait_ge(pv_ps, h * 4 + (n + 1))
                    o.step(act.activation(SG[:, 0, :], AUX[:, PV_BANK[t], :], ACT.Square, accum_out=so[:, n:n + 1]))
                    act.activation(sd_o[:, n:n + 1], so[:, n:n + 1], ACT.Sqrt, bias=eps, scale=1.0 / RV).then_inc(o_rms, 1)
                hi(6)
                hi(7)
                for t in range(TT):
                    act.wait_ge(pe_steps, fin(h * HEAD_SPLIT + 5, t))
                    if t >= 2:
                        act.wait_ge(y_done, h * 4 + (t - 1))
                    act.activation(SG[:, t % 2, :], ACC[:, t, :], ACT.Silu).then_inc(silu_done, 1)
                    if t:
                        head_y_hi(act, h, t - 1)
                head_y_hi(act, h, TT - 1)
                split_hi(act, 0, 0, *after_head(h)[:2])
                o.leave(RH)
            def moe(layer, n0):
                if layer == 0:
                    first_hi(act, layer, n0, [1])
                moe_norm_act(act, 1 if layer == 0 else 4, o)
                first_hi(act, layer, n0, [2, 3])
                route_act(act, layer)
                base = 0 if layer == 0 else n0
                token_rows(act, base + layer)
                tokens_hi(act, base + layer)
                s0 = moe_s(layer, n0)
                n, N = blocks(act, layer, n0, lambda b, B, first: expert_act(act, layer, n0, s0, b, B, first))
                y_out_act(act, n * MOE_CHUNKS + s0 - 1, N - 1)
                if layer == 0:
                    for m in range(3):
                        kv_hi(act, N, m)
                combine_act(act, layer, o)
                return N
            n0 = moe(0, None)
            s0 = moe_s(1, n0) - MIX_CHUNKS
            a0 = n0 * 3 + (C_MOE0 // RING)
            for u in range(4):
                for m in ([3], [4, 5], [6, 7], [8, 9])[u]:
                    kv_hi(act, n0, m)
                if u < 2:
                    qk_norm_act(act, u, u, s0 + 2 * u + 1, kn_g, lambda t, u=u: KT[:, 4 * u:4 * u + 4, t * P:(t + 1) * P], None)
                    if u == 1:
                        act.wait_ge(lam_sum, 1)
                        act.activation(lam_s[:, 2:4], lam_s[:, 0:2], ACT.Exp).then_inc(lam_exp, 1)
                else:
                    for t in range(TT):
                        act.wait_ge(pe_steps, fin(s0 + 2 * u + 1, t))
                        act.activation(VV[:, t, (u - 2) * 512:(u - 1) * 512], ACC[:, t, :], ACT.Copy).then_inc(acc_free, 1)
            norm_act_hi(act, 3)
            with act.Fori(0, 2) as g:
                def hi(i):
                    slot, arrived = mix_pos(g + i // 4, i % 4)
                    split_hi(act, slot, i % RING, arrived + a0, free_steps(g * 4 + s0 + (8 + i)))
                o.enter(g, len(UNITS))
                qk_norm_act(act, g + 2, None, g * 4 + s0 + 9, qn8, lambda t: QT[:, :, t * P:(t + 1) * P], g * 8 + 36)
                hi(2)
                hi(3)

                def exps(u):
                    p, vis = u % 2, (UNITS[u][1] + 1) * P
                    act.wait_ge(s_max, g * 16 + (u + 1))
                    for t in range(2):
                        if t == 0 and u >= 3:
                            act.wait_ge(s_o, g * 16 + (u - 2))
                        act.activation(EE[u % 3][:, t, 0:vis], ACC[:, 2 * p + t, 0:vis], ACT.Exp, bias=att[:, 2 * p + t:2 * p + t + 1],
                                       scale=1.0, accum_out=att[:, 4 + 2 * p + t:5 + 2 * p + t]).then_inc(s_exp, 1)

                def copy_T(u):
                    p, vis = u % 2, (UNITS[u][1] + 1) * P
                    act.wait_ge(s_aT, g * 16 + (u + 1))
                    act.activation(EE[u % 3][:, 1, 0:vis], AUX[:, p, 0:vis], ACT.Copy).then_inc(s_at, 1)

                def take_out(u):
                    p, (j, qb) = u % 2, UNITS[u]
                    inv = att[:, 8 + 2 * (u % 4):9 + 2 * (u % 4)]
                    act.wait_ge(s_o, g * 16 + (u + 1))
                    act.activation(OUT[:, qb, j, :], AUX[:, 2 + p, 0:P], ACT.Copy, scale=inv)
                    o.step(act.activation(JUNK, AUX[:, 2 + p, 0:P], ACT.Square, scale=inv, accum_out=out_ms[:, u:u + 1]))
                    act.sem_inc(s_out, 1)
                for u in range(len(UNITS) + 2):
                    if u < len(UNITS):
                        exps(u)
                    if 1 <= u <= len(UNITS):
                        copy_T(u - 1)
                    if u >= 2:
                        take_out(u - 2)
                act.activation(out_rms, out_ms, ACT.Sqrt, bias=eps, scale=1.0 / P).then_inc(s_root, 1)
                for t in range(TT):
                    act.wait_ge(s_oT, g * 4 + (t + 1))
                    act.activation(bview(BH)[:, :, t * P:(t + 1) * P], AUX[:, t % 2, :].rearrange("p (k c) -> p k c", c=P),
                                   ACT.Copy, scale=subln).then_inc(s_ohi, 1)
                for i in range(2):
                    hi(4 + i)
                o.leave(2)
            moe(1, n0)

        @block.tensor
        def _(pe):
            pe.wait_ge(started, 1)
            pe.wait_ge(table_in, 16)
            for q in range(4):
                ada_sum(pe, q, q % 2)
            for t in range(TT):
                norm_pe(pe, 0, t)
            pe.wait_ge(n_lo, TT)
            with pe.Fori(0, RH) as h:
                S = h * HEAD_SPLIT

                def C(i):
                    return head_pos(h, AT_SPLIT[i])[0]

                def q_of(j):
                    return h * 6 + (4 + j)

                def after_qk(q, t):
                    if q == 1 and t == 3:
                        ada_sum(pe, q_of(0), 0)

                def before_v(t):
                    pe.wait_ge(rot_done, h * 4 + (t + 1))
                    if t >= 2:
                        pe.wait_ge(qk_out, h * 4 + (t - 1))
                    for j in range(4):
                        last = nc.tensor.transpose(AUX[:, t % 2, j * P:(j + 1) * P], QKR[:, t % 2, j * P:(j + 1) * P], ident)
                    last.then_inc(qk_T, 1)

                def after_v(q, t):
                    if (q, t) in ((0, 3), (1, 1)):
                        ada_sum(pe, q_of(1 + q), 1 - q)

                def y_T_(t):
                    pe.wait_ge(y_done, h * 4 + (t + 1))
                    if t >= 2:
                        pe.wait_ge(y_lo, h * 4 + (t - 1))
                    for k in range(4):
                        last = nc.tensor.transpose(AUX[:, t % 2, k * P:(k + 1) * P], V1[:, t, k * P:(k + 1) * P], ident)
                    last.then_inc(y_T, 1)

                def after_g(q, t):
                    if q == 0 and t == 3:
                        ada_sum(pe, q_of(4), 0)
                    if q == 1 and t:
                        y_T_(t - 1)

                project(pe, (S, 0), (C(0), C(1)), h * 5, hT(AH), hT(AL), after_qk, halves=2)
                project(pe, (S, 2), (C(2), C(3)), h * 5 + 1, hT(AH), hT(AL), after_v, before=before_v)
                pe.wait_ge(qk_out, h * 4 + 4)
                for m in range(TT):
                    if m == 3:
                        pe.wait_ge(st_done, h * 4 + 1)
                    n = T - m * P
                    for k in range(2):
                        last = nc.tensor.matmul(AUX[:, m % 3, 0:n], qkT[:, 2 + k, m * P:(m + 1) * P], qkT[:, k, m * P:T],
                                                start=(k == 0), stop=(k == 1))
                    last.then_inc(st_ps, 1)
                pe.wait_ge(st_done, h * 4 + 4)
                pe.wait_ge(acc_free, h * 20 + 12)
                for t in reversed(range(TT)):
                    if t == 0:
                        pe.wait_ge(o_norm, h * 4 + 1)
                    for m in range(t + 1):
                        at_ = ST_AT[m] + (t - m) * P
                        last = nc.tensor.matmul(AUX[:, PV_BANK[t], :], ST[:, at_:at_ + P], V1[:, m, :],
                                                start=(m == 0), stop=(m == t))
                    last.then_inc(pv_ps, 1)
                ada_sum(pe, q_of(3), 1)
                project(pe, (S, 4), (C(4), C(5)), h * 5 + 2, hT(AH), hT(AL), after_g)

                def out_ready(t):
                    if t == 1:
                        y_T_(3)
                    pe.wait_ge(y_lo, h * 4 + (t + 1))
                for q in range(2):
                    out_project(pe, 6 + q, C(6 + q), h * 5 + (3 + q), q, out_ready if q == 0 else None)
                    if q == 0:
                        ada_sum(pe, q_of(5), 1)
            def moe(layer, n0):
                moe_norm_pe(pe, 1 if layer == 0 else 4)
                route_pe(pe, layer)
                base = 0 if layer == 0 else n0
                pe.wait_ge(routed, layer + 1)
                pe.wait_ge(n_lo, TT * (2 if layer == 0 else 5))
                pick_tokens(pe, base + layer, 0)
                pick_tokens(pe, base + layer, 1)
                transpose_tokens(pe, base + layer)
                c0, s0 = moe_c(layer, n0), moe_s(layer, n0)
                return blocks(pe, layer, n0, lambda b, B, first: expert_pe(pe, layer, c0, s0, b, B))[1]
            n0 = moe(0, None)
            before = normed(pe, 2)
            c0, s0 = moe_c(1, n0) - MIX_CHUNKS, moe_s(1, n0) - MIX_CHUNKS
            for u in range(4):
                project(pe, (s0, 2 * u), (c0 + 2 * u, c0 + 2 * u + 1), 20 + u, hT(AH), hT(AL),
                        before=before if u == 0 else None)
                if u < 2:
                    qk_norm_pe(pe, u, 20 + u)
            for t in range(TT):
                norm_pe(pe, 3, t)
            pe.wait_ge(n_lo, TT * 4)
            with pe.Fori(0, 2) as g:
                w = g * 3 + 24
                U0 = g * 16
                project(pe, (s0, 0), (g * 4 + c0 + 8, g * 4 + c0 + 9), w, hT(AH), hT(AL))
                qk_norm_pe(pe, g + 2, w)
                pe.wait_ge(acc_free, w * 4 + 8)

                def scores(u):
                    p, (j, qb) = u % 2, UNITS[u]
                    vis = (qb + 1) * P
                    if j == 0:
                        pe.wait_ge(a_kv, g * 4 + (9 + qb))
                    if qb == 0:
                        pe.wait_ge(ks_in, g * 4 + (j + 1))
                    if u >= 2:
                        pe.wait_ge(s_exp, g * 32 + 2 * (u - 1))
                    for t in range(2):
                        rows = slice(t * HD, (t + 1) * HD)
                        last = nc.tensor.matmul(ACC[:, 2 * p + t, 0:vis], QT[rows, j, qb * P:(qb + 1) * P], KS[j % 2][rows, 0:vis],
                                                start=True, stop=True)
                    last.then_inc(s_ps, 1)

                def a_T_(u):
                    p, (j, qb) = u % 2, UNITS[u]
                    pe.wait_ge(s_a, U0 + (u + 1))
                    if u >= 2:
                        pe.wait_ge(s_at, U0 + (u - 1))
                    for k in range(qb + 1):
                        last = nc.tensor.transpose(AUX[:, p, k * P:(k + 1) * P], EE[u % 3][:, 0, k * P:(k + 1) * P], ident)
                    last.then_inc(s_aT, 1)

                def pv(u):
                    p, (j, qb) = u % 2, UNITS[u]
                    pe.wait_ge(s_at, U0 + (u + 1))
                    if u >= 2:
                        pe.wait_ge(s_out, U0 + (u - 1))
                    for k in range(qb + 1):
                        v = VV[:, k, ds(g * 512 + j * P, P)]
                        last = nc.tensor.matmul(AUX[:, 2 + p, 0:P], EE[u % 3][:, 1, k * P:(k + 1) * P], v,
                                                start=(k == 0), stop=(k == qb))
                    last.then_inc(s_o, 1)

                def o_T(t):
                    pe.wait_ge(s_on, g * 4 + (t + 1))
                    if t >= 2:
                        pe.wait_ge(s_olo, g * 4 + (t - 1))
                    for j in range(4):
                        last = nc.tensor.transpose(AUX[:, t % 2, j * P:(j + 1) * P], ON[:, t % 2, j, :], ident)
                    last.then_inc(s_oT, 1)
                scores(0)
                scores(1)
                for u in range(len(UNITS)):
                    a_T_(u)
                    if u + 2 < len(UNITS):
                        scores(u + 2)
                    pv(u)
                for t in range(TT):
                    o_T(t)
                for q in range(2):
                    out_project(pe, 2 + q, g * 4 + c0 + (10 + q), w + (1 + q), q,
                                (lambda t: pe.wait_ge(s_olo, g * 4 + (t + 1))) if q == 0 else None)
            moe(1, n0)

        @block.vector
        def _(dve):
            o = Own(dve, "dve")
            o.step(dve.memset(ONES[:, :], 1.0))
            o.step(dve.memset(eps, EPS))
            dve.memset(credit, 0.0).then_inc(raw_used, RING)
            dve.sem_inc(pe_steps, 4 * RING)
            dve.sem_inc(acc_free, TT)
            dve.sem_inc(out_free, 1)
            dve.sem_inc(started, 3)
            dve.wait_ge(cact_done, 1)
            for q in range(4):
                ada_acc(dve, o, q, q % 2, [(2 * q) % RING, (2 * q + 1) % RING], [(2 * q) // RING + 1, (2 * q + 1) // RING + 1])
                if q:
                    ada_row(dve, q - 1)
            ada_row(dve, 3)
            norm_dve(dve, 0, o)
            HEAD_STEPS = 6 * 8 + 8 + 4 + 8
            split_lo(dve, 0, 0, C_HEAD // RING + 1, 4, 1)
            with dve.Fori(0, RH) as h:
                o.enter(h, HEAD_STEPS)

                def lo(i):
                    _, slot, arrived = head_pos(h, AT_SPLIT[i])
                    split_lo(dve, slot, i % RING, arrived, free_steps(h * HEAD_SPLIT + i), h * HEAD_SPLIT + (i + 1))

                def ada(j):
                    q = h * 6 + (4 + j)
                    pos = [head_pos(h, i) for i in AT_ADA[j]]
                    ada_acc(dve, o, q, j % 2, [x[1] for x in pos], [x[2] for x in pos])

                def arow(j):
                    ada_row(dve, h * 6 + (4 + j))
                ada(0)
                lo(1)
                ada(1)
                lo(2)
                for t in range(TT):
                    dve.wait_ge(pe_steps, fin(h * HEAD_SPLIT + 1, t))
                    if t == 0:
                        dve.wait_ge(rope_in, 32)
                    x4 = ACC[:, t, :].rearrange("p (z d) -> p z d", d=P)
                    cs = row(ROPE[:, 0, t, :], 4)
                    sn = row(ROPE[:, 1, t, :], 4)
                    a4, b4 = (ROT[:, i, :].rearrange("p (z d) -> p z d", d=P) for i in range(2))
                    dve.tensor_tensor(a4, x4, cs, ALU.mult)
                    o.step(dve.tensor_tensor(b4, x4, sn, ALU.mult))
                    dve.sem_inc(acc_free, 1)
                    if t >= 2:
                        dve.wait_ge(qk_T, h * 4 + (t - 1))
                    r = QKR[:, t % 2, :].rearrange("p (z s d) -> p z s d", s=2, d=P)
                    a2, b2 = (ROT[:, i, :].rearrange("p (z s d) -> p z s d", s=2, d=P) for i in range(2))
                    dve.tensor_tensor(r[:, :, 0, :], a2[:, :, 0, :], b2[:, :, 1, :], ALU.subtract)
                    o.step(dve.tensor_tensor(r[:, :, 1, :], a2[:, :, 1, :], b2[:, :, 0, :], ALU.add))
                    dve.sem_inc(rot_done, 1)
                arow(0)
                ada(2)
                lo(3)
                arow(1)
                ada(3)
                lo(4)
                arow(2)
                ada(4)
                dve.wait_ge(head_in, h * 32 + 32)
                for m in range(TT):
                    dve.wait_ge(st_ps, h * 4 + (m + 1))
                    n = T - m * P
                    dve.tensor_tensor(ST[:, ST_AT[m]:ST_AT[m] + n], AUX[:, m % 3, 0:n], DEC[:, 0:n], ALU.mult).then_inc(st_done, 1)
                for n, t in enumerate(reversed(range(TT))):
                    dve.wait_ge(o_rms, h * 4 + (n + 1))
                    o.step(dve.reciprocal(sd_o[:, n:n + 1], sd_o[:, n:n + 1]))
                    dve.scalar_tensor_tensor(V1[:, t, :], AUX[:, PV_BANK[t], :], sd_o[:, n:n + 1], GN, ALU.mult,
                                             ALU.mult).then_inc(o_norm, 1)
                lo(5)
                arow(3)
                ada(5)
                lo(6)
                arow(4)
                dve.wait_ge(o_norm, h * 4 + 4)
                for t in range(TT):
                    dve.wait_ge(silu_done, h * 4 + (t + 1))
                    dve.tensor_tensor(V1[:, t, :], V1[:, t, :], SG[:, t % 2, :], ALU.mult).then_inc(y_done, 1)
                    dve.sem_inc(acc_free, 1)
                    if t:
                        head_y_lo(dve, h, t - 1)
                head_y_lo(dve, h, TT - 1)
                lo(7)
                dve.wait_ge(gate_in, 16)
                for q in range(2):
                    if q == 1:
                        arow(5)
                        split_lo(dve, 0, 0, *after_head(h))
                    for t in range(TT):
                        residual_add(dve, o, fin(h * HEAD_SPLIT + (6 + q), t), q, t, GATE, TMP)
                o.leave(RH)
            def moe(layer, n0, gate_count):
                moe_norm_dve(dve, 1 if layer == 0 else 4, o)
                if layer == 0:
                    first_lo(dve, layer, n0, [1])
                route_dve(dve, layer, o)
                first_pick(dve, o)
                route_rest_dve(dve, layer, o)
                first_lo(dve, layer, n0, [2, 3])
                base = 0 if layer == 0 else n0
                tokens_lo(dve, base + layer)
                c0, s0 = moe_c(layer, n0), moe_s(layer, n0)
                n, N = blocks(dve, layer, n0, lambda b, B, first: expert_dve(dve, layer, n0, c0, s0, b, B, first))
                y_out_dve(dve, n * MOE_CHUNKS + s0 - 1, N - 1)
                if layer == 0:
                    for m in range(3):
                        kv_lo(dve, N, m)
                combine_dve(dve, layer, o, gate_count)
                return N
            n0 = moe(0, None, 2)
            s0 = moe_s(1, n0) - MIX_CHUNKS
            a0 = n0 * 3 + (C_MOE0 // RING)
            for u in range(4):
                if u == 3:
                    for t in range(2):
                        norm_dve_rows(dve, 3, t, o)
                for m in ([3], [4, 5], [6, 7], [8, 9])[u]:
                    kv_lo(dve, n0, m)
                if u < 2:
                    qk_norm_dve(dve, u, o)
                if u == 1:
                    dve.wait_ge(lam_in, 16)
                    for i in range(2):
                        o.step(dve.tensor_tensor(LAMT, LAMV[:, 2 * i * HD:(2 * i + 1) * HD], LAMV[:, (2 * i + 1) * HD:(2 * i + 2) * HD],
                                                 ALU.mult))
                        o.step(dve.tensor_reduce(lam_s[:, i:i + 1], LAMT, AX.X, ALU.add))
                    dve.wait_ge(cols_in, 16 * 5)
                    o.step(dve.tensor_scalar(qn8, qn, HD ** -0.5, None, ALU.mult))
                    dve.sem_inc(lam_sum, 1)
            dve.wait_ge(lam_exp, 1)
            o.step(dve.tensor_tensor(nlam, lam_s[:, 3:4], lam_s[:, 2:3], ALU.subtract))
            o.step(dve.tensor_scalar(nlam, nlam, -LAMBDA_INIT, None, ALU.add))
            norm_dve(dve, 3, o, early=2)
            with dve.Fori(0, 2) as g:
                def lo(i):
                    slot, arrived = mix_pos(g + i // 4, i % 4)
                    S = g * 4 + s0 + (8 + i)
                    split_lo(dve, slot, i % RING, arrived + a0, free_steps(S), S + 1)
                o.enter(g, QK_STEPS + 3 * len(UNITS) + 2 + 8)
                qk_norm_dve(dve, g + 2, o)
                lo(2)
                lo(3)

                def maxima(u):
                    p, vis = u % 2, (UNITS[u][1] + 1) * P
                    dve.wait_ge(s_ps, g * 16 + (u + 1))
                    o.step(dve.memset(ACC[0:CHUNK, 2 * p:2 * p + 2, vis - CHUNK:vis], -BIG))
                    dve.tensor_reduce(att[:, 2 * p:2 * p + 2], ACC[:, 2 * p:2 * p + 2, 0:vis], AX.X, ALU.max,
                                      negate=True).then_inc(s_max, 1)

                def mix(u):
                    p, vis = u % 2, (UNITS[u][1] + 1) * P
                    sums, r = att[:, 4 + 2 * p:6 + 2 * p], att[:, 8 + 2 * (u % 4):10 + 2 * (u % 4)]
                    dve.wait_ge(s_exp, g * 32 + (2 * u + 2))
                    o.step(dve.reciprocal(r, sums))
                    o.step(dve.scalar_tensor_tensor(r[:, 1:2], r[:, 1:2], nlam, sums[:, 0:1], ALU.mult, ALU.mult))
                    dve.scalar_tensor_tensor(EE[u % 3][:, 0, 0:vis], EE[u % 3][:, 1, 0:vis], r[:, 1:2], EE[u % 3][:, 0, 0:vis],
                                             ALU.mult, ALU.add).then_inc(s_a, 1)

                def o_norm_(t):
                    if t >= 2:
                        dve.wait_ge(s_oT, g * 4 + (t - 1))
                    inv = out_rms.rearrange("p (j q) -> p q j", q=TT)[:, t, :]
                    dve.tensor_tensor(ON[:, t % 2, :, :], OUT[:, t, :, :], col(inv, P), ALU.mult).then_inc(s_on, 1)

                def o_lo(t):
                    dve.wait_ge(s_ohi, g * 4 + (t + 1))
                    dve.scalar_tensor_tensor(bview(BL)[:, :, t * P:(t + 1) * P], AUX[:, t % 2, :].rearrange("p (k c) -> p k c", c=P),
                                             subln, bview(BH)[:, :, t * P:(t + 1) * P].bitcast(F32),
                                             ALU.mult, ALU.subtract).then_inc(s_olo, 1)
                maxima(0)
                maxima(1)
                mix(0)
                for u in range(1, len(UNITS)):
                    mix(u)
                    if u + 1 < len(UNITS):
                        maxima(u + 1)
                dve.wait_ge(s_root, g + 1)
                o.step(dve.reciprocal(out_rms, out_rms))
                o.step(dve.tensor_scalar(out_rms, out_rms, 1.0 - LAMBDA_INIT, None, ALU.mult))
                for t in range(TT):
                    o_norm_(t)
                    if t:
                        o_lo(t - 1)
                o_lo(TT - 1)
                dve.sem_inc(out_free, 1)
                dve.wait_ge(gate_in, g * 16 + 48)
                for q in range(2):
                    lo(4 + q)
                    for t in range(TT):
                        residual_add(dve, o, fin(g * 4 + s0 + (10 + q), t), q, t, GATE2, TMP2)
                o.leave(2)
            moe(1, n0, 5)


_INS = ["x", "c", "ada_w", "ada_b", "norm_mix", "norm_ffn", "ret_w_in", "ret_gn", "ret_w_out", "kv_ada_w", "kv_ada_b",
        "kv_norm", "kv_w", "k_norm", "diff_w_q", "q_norm", "diff_lam", "diff_subln", "diff_w_out", "moe_w_group",
        "moe_b_group", "moe_w_expert", "moe_b_expert", "moe_w1", "moe_w3", "moe_w2"]


def kernel(**inputs):
    import concourse.bacc as bacc
    from concourse.bass_utils import run_bass_kernel_spmd

    nc = bacc.Bacc("TRN2", target_bir_lowering=False, num_devices=1)
    arrays, io = {}, {}
    for name, a in [(n, inputs[n]) for n in _INS] + list(shape_constants().items()):
        a = np.ascontiguousarray(a)
        arrays[f"in_{name}"] = a
        io[name] = nc.dram_tensor(f"in_{name}", a.shape, mybir.dt.from_np(a.dtype), kind="ExternalInput").ap()
    out = nc.dram_tensor("out_x", (1, T, D), F32, kind="ExternalOutput").ap()
    build_trunk(nc, io, out)
    r = run_bass_kernel_spmd(nc, [arrays], core_ids=[0])
    return r.results[0]["out_x"]
```
